# Optimizing a Trainium2 kernel written in Bass

```python
import math
import jax, jax.numpy as jnp
from jax import lax
import numpy as np

D_MODEL = 1024
BATCH = 1
SEQ = 1024
DEPTH = 2

N_MIXERS = 3
EPS = 1e-6
NEG_BIG = -1e30

POOL_WINDOWS = (2, 4, 8, 16)
POOL_WIDTH = 2 * D_MODEL
POOL_GROUP = POOL_WIDTH // len(POOL_WINDOWS)

ATT_GROUPS = ((128, 1), (512, 4), (2048, 16))
ATT_HEAD_DIM = 128
ATT_HEADS = D_MODEL // ATT_HEAD_DIM
ATT_WIDTH = ATT_HEADS * ATT_HEAD_DIM
ROPE_DIM = ATT_HEAD_DIM // 4
ROPE_THETA = 500000.0

RET_HEADS = 4
RET_QK_DIM = D_MODEL // RET_HEADS
RET_V_DIM = 2 * D_MODEL // RET_HEADS
RET_QK = RET_HEADS * RET_QK_DIM
RET_V = RET_HEADS * RET_V_DIM
RET_CHUNK = 128
RET_THETA = 10000.0
RET_DECAY_BASE = 5.0

N_POOL_LAYERS = len(range(0, DEPTH, N_MIXERS))
N_ATT_LAYERS = len(range(1, DEPTH, N_MIXERS))
N_RET_LAYERS = len(range(2, DEPTH, N_MIXERS))

kernel_name = "hybrid_pool_dilattn_retention_encoder"

F32 = jnp.float32

def rms_norm(x, w):
    x32 = x.astype(F32)
    y = x32 * lax.rsqrt(jnp.mean(x32 * x32, axis=-1, keepdims=True) + EPS)
    return (y * w.astype(F32)).astype(x.dtype)

def rotary(x, pos, rot_dim, theta):
    half = rot_dim // 2
    inv_freq = 1.0 / (theta ** (jnp.arange(half, dtype=F32) * 2.0 / rot_dim))
    ang = pos.astype(F32)[:, None] * inv_freq[None, :]
    cos = jnp.cos(ang)[None, :, None, :]
    sin = jnp.sin(ang)[None, :, None, :]
    xr = x[..., :rot_dim].astype(F32)
    x1, x2 = xr[..., :half], xr[..., half:]
    rot = jnp.concatenate([x1 * cos - x2 * sin, x2 * cos + x1 * sin], axis=-1).astype(x.dtype)
    return jnp.concatenate([rot, x[..., rot_dim:]], axis=-1)

def centred_window_mean(u, window):
    B, S, C = u.shape
    cs = jnp.concatenate([jnp.zeros((B, 1, C), F32), jnp.cumsum(u.astype(F32), axis=1)], axis=1)
    t = jnp.arange(S)
    lo = jnp.clip(t - window // 2, 0, S)
    hi = jnp.clip(t - window // 2 + window, 0, S)
    count = (hi - lo).astype(F32)
    return (cs[:, hi] - cs[:, lo]) / count[None, :, None]

def pool_mixer(h, w_in, w_group, scale, w_out):
    B, S, _ = h.shape
    proj = h @ w_in
    u, gate = proj[..., :POOL_WIDTH], proj[..., POOL_WIDTH:]
    ug = u.reshape(B, S, len(POOL_WINDOWS), POOL_GROUP)
    pooled = jnp.stack([centred_window_mean(ug[:, :, g], w) for g, w in enumerate(POOL_WINDOWS)], axis=2)
    diff = (pooled - ug.astype(F32)).astype(h.dtype)
    mixed = jnp.einsum('bsgc,gcd->bsgd', diff, w_group).reshape(B, S, POOL_WIDTH) * scale
    return (mixed * jax.nn.silu(gate)) @ w_out

def dilated_window_attention(q, k, v, dilation, n_side):
    B, S, H, Dh = q.shape
    blk = n_side
    seg = dilation * blk
    Sp = -(-S // seg) * seg
    nblk = Sp // seg

    def to_sub(t):
        t = jnp.pad(t, ((0, 0), (0, Sp - S), (0, 0), (0, 0)))
        return t.reshape(B, nblk, blk, dilation, H, Dh).transpose(0, 3, 1, 2, 4, 5)

    def band(t):
        tp = jnp.pad(t, ((0, 0), (0, 0), (1, 1), (0, 0), (0, 0), (0, 0)))
        return jnp.concatenate([tp[:, :, :-2], tp[:, :, 1:-1], tp[:, :, 2:]], axis=3)

    qb = to_sub(q)
    kw, vw = band(to_sub(k)), band(to_sub(v))

    r = jnp.arange(dilation)[:, None, None]
    bidx = jnp.arange(nblk)[None, :, None]
    c = jnp.arange(3 * blk)
    key_sub = (bidx - 1) * blk + c[None, None, :]
    key_pos = key_sub * dilation + r
    key_ok = (key_sub >= 0) & (key_pos < S)
    offs = c[None, :] - blk - jnp.arange(blk)[:, None]
    band_ok = jnp.abs(offs) <= n_side
    mask = key_ok[:, :, None, :] & band_ok[None, None]

    scores = jnp.einsum('brnqhe,brnkhe->brnhqk', qb, kw).astype(F32) * (Dh ** -0.5)
    scores = jnp.where(mask[None, :, :, None], scores, NEG_BIG)
    m = jnp.max(scores, axis=-1, keepdims=True)
    p = jnp.exp(scores - m)
    den = jnp.sum(p, axis=-1, keepdims=True)
    o = jnp.einsum('brnhqk,brnkhe->brnhqe', p, vw.astype(F32)) / den
    lse = (m + jnp.log(den))[..., 0]
    o = o.transpose(0, 2, 4, 1, 3, 5).reshape(B, Sp, H, Dh)[:, :S]
    lse = lse.transpose(0, 2, 4, 1, 3).reshape(B, Sp, H)[:, :S]
    return o, lse

def dilated_attention_mixer(h, w_in, q_norm, k_norm, w_out):
    B, S, _ = h.shape
    n_g = len(ATT_GROUPS)
    proj = h @ w_in
    qkv = proj[..., :3 * n_g * ATT_WIDTH].reshape(B, S, n_g, 3, ATT_HEADS, ATT_HEAD_DIM)
    gate = proj[..., 3 * n_g * ATT_WIDTH:]
    pos = jnp.arange(S)
    outs, lses = [], []
    for g, (window, dil) in enumerate(ATT_GROUPS):
        q = rotary(rms_norm(qkv[:, :, g, 0], q_norm[g]), pos, ROPE_DIM, ROPE_THETA)
        k = rotary(rms_norm(qkv[:, :, g, 1], k_norm[g]), pos, ROPE_DIM, ROPE_THETA)
        o, lse = dilated_window_attention(q, k, qkv[:, :, g, 2], dil, window // (2 * dil))
        outs.append(o)
        lses.append(lse)
    weights = jax.nn.softmax(jnp.stack(lses, axis=0), axis=0)
    o = jnp.einsum('gbsh,gbshe->bshe', weights, jnp.stack(outs, axis=0))
    y = o.reshape(B, S, ATT_WIDTH).astype(h.dtype) * jax.nn.silu(gate)
    return y @ w_out

def retention_scan(q, k, v, log_gamma, include_diag):
    B, S, H, dk = q.shape
    dv = v.shape[-1]
    C = RET_CHUNK
    N = S // C

    def chunks(t):
        return t.astype(F32).reshape(B, N, C, H, t.shape[-1]).transpose(1, 0, 3, 2, 4)

    qc, kc, vc = chunks(q), chunks(k), chunks(v)
    i = jnp.arange(C, dtype=F32)
    diff = i[:, None] - i[None, :]
    keep = (diff >= 0) if include_diag else (diff > 0)
    inner_decay = jnp.where(keep[None], jnp.exp(jnp.where(keep, diff, 0.0)[None] * log_gamma[:, None, None]), 0.0)
    q_decay = jnp.exp((i + 1.0)[None, :] * log_gamma[:, None])[..., None]
    k_decay = jnp.exp((C - 1.0 - i)[None, :] * log_gamma[:, None])[..., None]
    chunk_decay = jnp.exp(C * log_gamma)[:, None, None]

    def step(state, inp):
        qi, ki, vi = inp
        inner = jnp.einsum('bhqd,bhkd->bhqk', qi, ki) * inner_decay
        out = jnp.einsum('bhqk,bhkv->bhqv', inner, vi) + jnp.einsum('bhqd,bhdv->bhqv', qi * q_decay, state)
        state = state * chunk_decay + jnp.einsum('bhkd,bhkv->bhdv', ki * k_decay, vi)
        return state, out

    _, out = lax.scan(step, jnp.zeros((B, H, dk, dv), F32), (qc, kc, vc))
    return out.transpose(1, 0, 3, 2, 4).reshape(B, S, H, dv)

def retention_mixer(h, w_in, decay_exp, w_out):
    B, S, _ = h.shape
    proj = h @ w_in
    qf, kf, qb, kb, v, gate = jnp.split(proj, [RET_QK, 2 * RET_QK, 3 * RET_QK, 4 * RET_QK, 4 * RET_QK + RET_V], axis=-1)
    pos = jnp.arange(S)
    scale = RET_QK_DIM ** -0.5

    def rot(t):
        return rotary(t.reshape(B, S, RET_HEADS, RET_QK_DIM), pos, RET_QK_DIM, RET_THETA)

    vh = v.reshape(B, S, RET_HEADS, RET_V_DIM)
    log_gamma = jnp.log1p(-jnp.exp2(-decay_exp.astype(F32)))
    fwd = retention_scan(rot(qf), rot(kf) * scale, vh, log_gamma[0], True)
    bwd = retention_scan(rot(qb)[:, ::-1], (rot(kb) * scale)[:, ::-1], vh[:, ::-1], log_gamma[1], False)[:, ::-1]
    y = fwd + bwd
    y = y * lax.rsqrt(jnp.mean(y * y, axis=-1, keepdims=True) + EPS)
    y = y.reshape(B, S, RET_V).astype(h.dtype) * jax.nn.silu(gate)
    return y @ w_out

def setup_inputs(seed: int = 0) -> dict:
    key = jax.random.key(seed)
    ks = jax.random.split(key, 20)
    n_g = len(ATT_GROUPS)

    def dense(k, shape, fan_in):
        return jax.random.normal(k, shape, F32) * (fan_in ** -0.5)

    def gain(k, shape):
        return 1.0 + 0.02 * jax.random.normal(k, shape, F32)

    x = jax.random.normal(ks[0], (BATCH, SEQ, D_MODEL), F32)
    pool_norm = gain(ks[1], (N_POOL_LAYERS, D_MODEL))
    pool_w_in = dense(ks[2], (N_POOL_LAYERS, D_MODEL, 2 * POOL_WIDTH), D_MODEL)
    pool_w_group = dense(ks[3], (N_POOL_LAYERS, len(POOL_WINDOWS), POOL_GROUP, POOL_GROUP), POOL_GROUP)
    pool_scale = gain(ks[4], (N_POOL_LAYERS, POOL_WIDTH))
    pool_w_out = dense(ks[5], (N_POOL_LAYERS, POOL_WIDTH, D_MODEL), POOL_WIDTH)
    att_norm = gain(ks[6], (N_ATT_LAYERS, D_MODEL))
    att_w_in = dense(ks[7], (N_ATT_LAYERS, D_MODEL, 3 * n_g * ATT_WIDTH + ATT_WIDTH), D_MODEL)
    att_q_norm = gain(ks[8], (N_ATT_LAYERS, n_g, ATT_HEAD_DIM))
    att_k_norm = gain(ks[9], (N_ATT_LAYERS, n_g, ATT_HEAD_DIM))
    att_w_out = dense(ks[10], (N_ATT_LAYERS, ATT_WIDTH, D_MODEL), ATT_WIDTH)
    ret_norm = gain(ks[11], (N_RET_LAYERS, D_MODEL))
    ret_w_in = dense(ks[12], (N_RET_LAYERS, D_MODEL, 4 * RET_QK + 2 * RET_V), D_MODEL)
    ret_decay = (RET_DECAY_BASE + jnp.arange(RET_HEADS, dtype=F32))[None, None, :] \
        + 0.1 * jax.random.normal(ks[13], (N_RET_LAYERS, 2, RET_HEADS), F32)
    ret_w_out = dense(ks[14], (N_RET_LAYERS, RET_V, D_MODEL), RET_V)
    return {"x": x,
            "pool_norm": pool_norm, "pool_w_in": pool_w_in, "pool_w_group": pool_w_group,
            "pool_scale": pool_scale, "pool_w_out": pool_w_out,
            "att_norm": att_norm, "att_w_in": att_w_in, "att_q_norm": att_q_norm,
            "att_k_norm": att_k_norm, "att_w_out": att_w_out,
            "ret_norm": ret_norm, "ret_w_in": ret_w_in, "ret_decay": ret_decay, "ret_w_out": ret_w_out}

def reference(x, pool_norm, pool_w_in, pool_w_group, pool_scale, pool_w_out,
              att_norm, att_w_in, att_q_norm, att_k_norm, att_w_out,
              ret_norm, ret_w_in, ret_decay, ret_w_out):
    for layer in range(DEPTH):
        kind, idx = layer % N_MIXERS, layer // N_MIXERS
        if kind == 0:
            h = rms_norm(x, pool_norm[idx])
            x = x + pool_mixer(h, pool_w_in[idx], pool_w_group[idx], pool_scale[idx], pool_w_out[idx])
        elif kind == 1:
            h = rms_norm(x, att_norm[idx])
            x = x + dilated_attention_mixer(h, att_w_in[idx], att_q_norm[idx], att_k_norm[idx], att_w_out[idx])
        else:
            h = rms_norm(x, ret_norm[idx])
            x = x + retention_mixer(h, ret_w_in[idx], ret_decay[idx], ret_w_out[idx])
    return x


_drawn_inputs = setup_inputs


def setup_inputs(seed=0):
    import zlib

    import numpy as np

    out = dict(_drawn_inputs(seed))
    spreads = {}
    factors = {'pool_norm': 3.948,
     'pool_scale': 6.204,
     'att_norm': 8.0,
     'att_q_norm': 8.0,
     'att_k_norm': 8.0}
    for name, (base, spread) in spreads.items():
        noise = np.random.default_rng([zlib.crc32(name.encode()), seed]).standard_normal(out[name].shape)
        drawn = base * np.exp(spread * noise) if base else spread * noise
        out[name] = __import__('jax').numpy.asarray(drawn.astype(out[name].dtype))
    for name, factor in factors.items():
        out[name] = (out[name] * factor).astype(out[name].dtype)
    return out
```

```python
from contextlib import ExitStack

import concourse.bass as bass
from concourse import mybir

F32 = mybir.dt.float32
F32R = mybir.dt.float32r
ALU = mybir.AluOpType
ACT = mybir.ActivationFunctionType
AX_X = mybir.AxisListType.X

P = 128
EPS = 1e-6
ROPE = 32
SIDE = 64
STRIDE = (1, 4, 8)
WINDOWS = (2, 4, 8, 16)
PAD = 8


def encoder_program(nc, x, pool_norm, pool_w_in, pool_w_group, pool_scale, pool_w_out, att_norm, att_w_in,
                    att_q_norm, att_k_norm, att_w_out, ident_d, mask0_d, mask1_d, mask2_d, cos_d, sin_d,
                    edge_d, out):
    T, D = x.shape[1], x.shape[2]
    TB, KD = T // P, D // P
    PW = pool_w_out.shape[1]
    NG = len(WINDOWS)
    GB = PW // NG // P
    HD = P
    H = D // HD
    NA = len(STRIDE)
    HALF = 4
    SCALE = float(HD) ** -0.5
    TPAD = T + SIDE
    KW = T + 2 * SIDE
    NCHUNK = (H // HALF) * NA

    x2 = x[0]
    out2 = out[0]
    w_in0, w_out0 = pool_w_in[0], pool_w_out[0]
    w_in1, w_out1 = att_w_in[0], att_w_out[0]

    x1_d = nc.dram_tensor("x1_spill", (T, D), F32, kind="Internal").ap()
    u_d = nc.dram_tensor("u_spill", (NA, H, P, T), F32, kind="Internal").ap()
    st_d = nc.dram_tensor("stat_spill", (NA, 2, H, T), F32, kind="Internal").ap()
    f_d = nc.dram_tensor("factor_spill", (NA, H, T), F32, kind="Internal").ap()

    def cols(w, j, n, k0, k):
        return w[k0 * P:(k0 + k) * P, j:j + n].rearrange("(k p) c -> p k c", p=P)

    units = []
    unit_of = {}

    def add(key, src, k, n):
        unit_of[key] = len(units)
        units.append((src, k, n))

    for g in range(NG):
        def wout_units(gg, pair):
            for i in range(2):
                add(("O", gg, pair, i), cols(w_out0, 0, D, gg * GB + 2 * pair + i, 1), 1, D)

        def wgroup_unit(pair):
            add(("M", g, pair), cols(pool_w_group[0, g], 256 * pair, 256, 0, GB), GB, 256)

        def win_unit(kind, c):
            add((kind, g, c), cols(w_in0, (g * GB + c) * P + (PW if kind == "G" else 0), P, 0, KD), KD, P)

        win_unit("U", 0)
        if g:
            wout_units(g - 1, 1)
        for c in range(1, GB):
            win_unit("U", c)
        win_unit("G", 0)
        wgroup_unit(0)
        win_unit("G", 1)
        win_unit("G", 2)
        wout_units(g, 0)
        wgroup_unit(1)
        win_unit("G", 3)
    wout_units(NG - 1, 1)
    UNITS0 = len(units)
    for half in range(H // HALF):
        for g in range(NA):
            for part in range(3):
                base = (g * 3 + part) * D + half * HALF * HD
                for i in range(4):
                    add(("A", half * NA + g, part, i), cols(w_in1, base, HALF * HD, 2 * i, 2), 2, HALF * HD)
    for h in range(H):
        add(("Y", h), cols(w_in1, 3 * NA * D + h * HD, P, 0, KD), KD, P)
    for hf in range(2):
        for i in range(4):
            add(("Z", hf, i), cols(w_out1, hf * 512, 512, 2 * i, 2), 2, 512)
    NU = len(units)
    R0, R1, RAW = 4, 6, 2

    def slot(u):
        return u % R0 if u < UNITS0 else (u - UNITS0) % R1

    ctx = ExitStack()
    with ctx:
        def sb(name, shape, dt, stack=ctx):
            return stack.enter_context(nc.sbuf_tensor(name, shape, dt))

        sems = {}

        def sem(name):
            if name not in sems:
                sems[name] = ctx.enter_context(nc.semaphore(name))
            return sems[name]

        hTh = sb("hTh", [P, KD, TPAD], F32R)
        hTl = sb("hTl", [P, KD, TPAD], F32R)
        raw = sb("raw", [P, RAW, 1024], F32)
        ident = sb("ident", [P, P], F32)
        zero = sb("zero", [P, 1], F32)
        edge = sb("edge", [P, NG, 2, 8], F32)
        pscale = sb("pscale", [P, PW // P], F32)
        ss = sb("ss", [P, TB], F32)
        var = sb("var", [P, TB], F32)
        root = sb("root", [P, TB], F32)
        tmp = sb("tmp", [P, TB], F32)
        rstd = sb("rstd", [P, TB], F32)
        with ExitStack() as l0:
            diffh = sb("diffh", [P, GB, T], F32R, l0)
            diffl = sb("diffl", [P, GB, T], F32R, l0)
            w0h = sb("w0h", [P, R0, 1024], F32R, l0)
            w0l = sb("w0l", [P, R0, 1024], F32R, l0)
            xs = sb("xs", [P, TB, D], F32, l0)
            zh = sb("zh", [P, 2, T], F32R, l0)
            zl = sb("zl", [P, 2, T], F32R, l0)
            bufU = sb("bufU", [P, T + 2 * PAD], F32, l0)
            bufS = sb("bufS", [P, T + 2 * PAD], F32, l0)
            bufG = sb("bufG", [P, T], F32, l0)
        with ExitStack() as l1:
            w1h = sb("w1h", [P, R1, 1024], F32R, l1)
            w1l = sb("w1l", [P, R1, 1024], F32R, l1)
            with ExitStack() as la:
                qT = sb("qT", [P, HALF, T], F32, la)
                kT = sb("kT", [P, HALF, KW], F32, la)
                vv = sb("vv", [P, TB, HALF * HD], F32, la)
                uo = sb("uo", [P, T], F32, la)
                qn = sb("qn", [P, 2, HALF * HD], F32, la)
                pp = sb("pp", [P, 2, 256], F32, la)
                pt = sb("pt", [P, 2, 256], F32, la)
                mask0 = sb("mask0", [P, 3, 256], F32, la)
                mask1 = sb("mask1", [P, 2, 256], F32, la)
                mask2 = sb("mask2", [P, P], F32, la)
                cosb = sb("cosb", [P, TB, ROPE], F32, la)
                sinb = sb("sinb", [P, TB, ROPE], F32, la)
                cosw = sb("cosw", [P, TB, ROPE], F32, la)
                sinw = sb("sinw", [P, TB, ROPE], F32, la)
                wrow = sb("wrow", [P, 2 * NA, ROPE], F32, la)
                wcol = sb("wcol", [P, 2 * NA], F32, la)
                ropeA = sb("ropeA", [P, HALF, ROPE], F32, la)
                ropeB = sb("ropeB", [P, HALF, ROPE], F32, la)
                stat = sb("stat", [P, 2, HALF, TB], F32, la)
                mmax = sb("mmax", [P, 2], F32, la)
                statT = sb("statT", [2 * HALF * TB, P], F32, la)
                qss = sb("qss", [P, HALF], F32, la)
                qvar = sb("qvar", [P, HALF], F32, la)
                qroot = sb("qroot", [P, HALF], F32, la)
                qtmp = sb("qtmp", [P, HALF], F32, la)
                qrstd = sb("qrstd", [P, HALF], F32, la)
            with ExitStack() as ly:
                yh = sb("yh", [P, H, T], F32R, ly)
                yl = sb("yl", [P, H, T], F32R, ly)
                uf = sb("uf", [P, 6, 512], F32, ly)
                gate = sb("gate", [P, 512], F32, ly)
                fm = sb("fm", [H * TB, NA, P], F32, ly)
                fden = sb("fden", [H * TB, NA, P], F32, ly)
                ftot = sb("ftot", [H * TB, P], F32, ly)

        pair = [ctx.enter_context(nc.psum_tensor(f"pair{i}", [P, 1024], F32)) for i in range(4)]

        def bank(i):
            return pair[i // 2][:, 512 * (i % 2):512 * (i % 2) + 512]

        def wview(u, lo):
            src, k, n = units[u]
            t = (w0l if lo else w0h) if u < UNITS0 else (w1l if lo else w1h)
            return t[:, slot(u), :].rearrange("p (k c) -> p k c", k=k)

        xin = [sem(f"xin{i}") for i in range(TB)]
        raw_in = [sem(f"raw_in{i}") for i in range(RAW)]
        w_hi, w_lo, w_used = sem("w_hi"), sem("w_lo"), sem("w_used")
        const_in, zero_set = sem("const_in"), sem("zero_set")
        nw_in = sem("nw_in")
        sq_done, var_done, root_done, xn_done = sem("sq_done"), sem("var_done"), sem("root_done"), sem("xn_done")
        xt_done, hhi_done, hlo_done, hpad_done = sem("xt_done"), sem("hhi_done"), sem("hlo_done"), sem("hpad_done")
        u_done, g_done, m_done, o_done = sem("u_done"), sem("g_done"), sem("m_done"), sem("o_done")
        u_copied, d_ready, dhi_done, diff_done = sem("u_copied"), sem("d_ready"), sem("dhi_done"), sem("diff_done")
        silu_done, z_ready, zhi_done, z_done, o_added = (sem("silu_done"), sem("z_ready"), sem("zhi_done"),
                                                         sem("z_done"), sem("o_added"))
        x1_out = sem("x1_out")
        acon_in, kpad_set, wcol_set = sem("acon_in"), sem("kpad_set"), sem("wcol_set")
        proj_done, qsq_done, qvar_done, qroot_done = (sem("proj_done"), sem("qsq_done"), sem("qvar_done"),
                                                      sem("qroot_done"))
        qn_done, rope_done, qt_done, qkT_done, v_done = (sem("qn_done"), sem("rope_done"), sem("qt_done"),
                                                         sem("qkT_done"), sem("v_done"))
        s_done, masked, m_ready, p_done, ptr_done, pt_ready, pv_done, u_evac, u_out = (
            sem("s_done"), sem("masked"), sem("m_ready"), sem("p_done"), sem("ptr_done"), sem("pt_ready"),
            sem("pv_done"), sem("u_evac"), sem("u_out"))
        stT_done, st_evac, st_out = sem("stT_done"), sem("st_evac"), sem("st_out")
        f_in, f_sub, f_exp, f_ready, f_out = sem("f_in"), sem("f_sub"), sem("f_exp"), sem("f_ready"), sem("f_out")
        uf_in, uf_used = sem("uf_in"), sem("uf_used")
        yg_done, ysilu_done, y_ready, yhi_done, y_done = (sem("yg_done"), sem("ysilu_done"), sem("y_ready"),
                                                          sem("yhi_done"), sem("y_done"))
        z1_done, out_ready = sem("z1_done"), sem("out_ready")
        x1_in = [sem(f"x1_in{i}") for i in range(3)]
        out_sent = [sem(f"out_sent{i}") for i in range(3)]
        dve_step, act_step, pool_step = sem("dve_step"), sem("act_step"), sem("pool_step")

        jobs = []
        for g in range(NG):
            jobs.append(("U", g, 0))
            if g:
                jobs += [("O", g - 1, 1, tb) for tb in range(TB)]
            jobs += [("U", g, c) for c in range(1, GB)]
            jobs += [("G", g, 0), ("M", g, 0), ("G", g, 1), ("M", g, 1), ("G", g, 2)]
            jobs += [("O", g, 0, tb) for tb in range(TB)]
            jobs += [("M", g, 2), ("G", g, 3), ("M", g, 3)]
        jobs += [("O", NG - 1, 1, tb) for tb in range(TB)]
        pair_of = {j: n % 4 for n, j in enumerate(jobs)}

        def released(job):
            kind, g = job[0], job[1]
            if kind == "U":
                return d_ready, GB * g + job[2] + 1
            if kind == "G":
                return silu_done, GB * g + job[2] + 1
            if kind == "M":
                return z_ready, GB * g + job[2] + 1
            return o_added, 2 * TB * g + TB * job[2] + job[3] + 1

        key_of = {n: key for key, n in unit_of.items()}

        def unit_released(u):
            key = key_of[u]
            kind, g = key[0], key[1]
            if kind == "U":
                return u_done, GB * g + key[2] + 1
            if kind == "G":
                return g_done, GB * g + key[2] + 1
            if kind == "M":
                return m_done, GB * g + 2 * key[2] + 2
            if kind == "O":
                return o_done, 2 * TB * g + TB * key[2] + TB
            if kind == "Y":
                return yg_done, g + 1
            n, i = (3 * g + key[2], key[3]) if kind == "A" else (3 * NCHUNK + g, key[2])
            if i < 3:
                return w_used, 3 * n + i + 1
            return (proj_done, TB * (n + 1)) if kind == "A" else (z1_done, TB * (g + 1))

        def mask_of(g, b):
            if g == 0:
                return mask0[:, 0 if b == 0 else (2 if b == TB - 1 else 1), :]
            return mask1[:, b % 2, :] if g == 1 else mask2[:, :]

        def key_cols(g, b):
            if g == 0:
                return P * b, 256
            if g == 1:
                return SIDE + 256 * (b // 2), 256
            return SIDE + P * b, P

        def value_blocks(g, b):
            return [(b - 1) % TB, b] if g == 0 else ([b - b % 2, b - b % 2 + 1] if g == 1 else [b])

        def value_tokens(t, kd, g, b):
            if g == 0:
                return t[:, kd, P * b + SIDE:P * b + SIDE + P]
            if g == 1:
                s = b // 2 + 4 * P * (b % 2)
                return t[:, kd, s:s + 4 * (P - 1) + 1:4]
            return t[:, kd, b:b + 8 * (P - 1) + 1:8]

        block = ctx.enter_context(nc.Block())

        @block.sync
        def _(sp):
            for u, (src, k, n) in enumerate(units):
                if u >= RAW:
                    sp.wait_ge(w_lo, u - RAW + 1)
                sp.dma_start(raw[:, u % RAW, :].rearrange("p (k c) -> p k c", k=k), src).then_inc(raw_in[u % RAW], 16)

        @block.gpsimd
        def _(pool):
            nc.gpsimd.memset(zero[:, :], 0.0).then_inc(zero_set, 1)
            pool.wait_ge(zero_set, 1)
            for u in range(NU):
                pool.wait_ge(raw_in[u % RAW], 16 * (u // RAW + 1))
                if u < UNITS0:
                    if u >= R0:
                        pool.wait_ge(*unit_released(u - R0))
                    hi, lo = w0h[:, slot(u), :], w0l[:, slot(u), :]
                else:
                    pool.wait_ge(*unit_released(max(UNITS0 - 1, u - R1)))
                    hi, lo = w1h[:, slot(u), :], w1l[:, slot(u), :]
                r = raw[:, u % RAW, :]
                nc.gpsimd.tensor_tensor(hi, r, zero[:, 0:1].to_broadcast([P, 1024]), ALU.add).then_inc(w_hi, 1)
                pool.wait_ge(w_hi, u + 1)
                nc.gpsimd.tensor_tensor(lo, r, hi.bitcast(F32), ALU.subtract).then_inc(w_lo, 1)

        @block.tensor
        def _(pe):
            def three(out, lh, ll, rh, rl, first, last):
                nc.tensor.matmul(out, lh, rh, start=first, stop=False)
                nc.tensor.matmul(out, lh, rl, start=False, stop=False)
                return nc.tensor.matmul(out, ll, rh, start=False, stop=last)

            def transpose_x(layer):
                for tb in range(TB):
                    n = layer * TB + tb
                    pe.wait_ge(xn_done, n + 1)
                    if tb >= 2:
                        pe.wait_ge(hlo_done, n - 1)
                    elif layer == 1:
                        pe.wait_ge(o_added, 2 * TB * NG - 2 + tb)
                    buf = (bufU, bufS)[tb % 2]
                    for kd in range(KD):
                        last = nc.tensor.transpose(pair[tb % 2][:, kd * P:kd * P + P],
                                                   buf[:, kd * P:kd * P + P], ident[:, :])
                    last.then_inc(xt_done, 1)

            def features_by_tokens(u, pr, kdn, rh, rl, col=0):
                wh, wl = wview(u, False), wview(u, True)
                for kd in range(kdn):
                    for hf in range(2):
                        last = three(pair[pr][:, 512 * hf:512 * hf + 512], wh[:, kd, col:col + P],
                                     wl[:, kd, col:col + P], rh(kd, hf), rl(kd, hf), kd == 0, kd == kdn - 1)
                return last

            def tok(t):
                return lambda kd, hf: t[:, kd, 512 * hf:512 * hf + 512]

            pe.wait_ge(const_in, 16 * 3)
            transpose_x(0)
            pe.wait_ge(hlo_done, TB)
            for n, job in enumerate(jobs):
                if n >= 4:
                    pe.wait_ge(*released(jobs[n - 4]))
                kind, g = job[0], job[1]
                pr = n % 4
                if kind in "UG":
                    u = unit_of[job]
                    pe.wait_ge(w_lo, u + 1)
                    last = features_by_tokens(u, pr, KD, tok(hTh), tok(hTl))
                    last.then_inc(u_done if kind == "U" else g_done, 1)
                elif kind == "M":
                    c = job[2]
                    u = unit_of[("M", g, c // 2)]
                    pe.wait_ge(w_lo, u + 1)
                    pe.wait_ge(diff_done, GB * (g + 1))
                    last = features_by_tokens(u, pr, GB, tok(diffh), tok(diffl), P * (c % 2))
                    last.then_inc(m_done, 1)
                else:
                    po, tb = job[2], job[3]
                    us = [unit_of[("O", g, po, i)] for i in range(2)]
                    if tb == 0:
                        pe.wait_ge(w_lo, us[1] + 1)
                        pe.wait_ge(z_done, GB * g + 2 * po + 2)
                    for i in range(2):
                        for hf in range(2):
                            last = three(pair[pr][:, 512 * hf:512 * hf + 512], zh[:, i, P * tb:P * tb + P],
                                         zl[:, i, P * tb:P * tb + P], wview(us[i], False)[:, 0, 512 * hf:512 * hf + 512],
                                         wview(us[i], True)[:, 0, 512 * hf:512 * hf + 512], i == 0, i == 1)
                    last.then_inc(o_done, 1)

            transpose_x(1)
            pe.wait_ge(hpad_done, 2)
            pe.wait_ge(hlo_done, 2 * TB)

            def project(c, n):
                part, tb = n // TB, n % TB
                t = c * 3 * TB + n
                if t >= 2:
                    before = n - 2 if n >= 2 else n - 2 + 3 * TB
                    cc = c if n >= 2 else c - 1
                    if before < 2 * TB:
                        pe.wait_ge(qn_done, 2 * TB * cc + before + 1)
                    else:
                        pe.wait_ge(v_done, TB * cc + before - 2 * TB + 1)
                if tb == 0:
                    pe.wait_ge(w_lo, unit_of[("A", c, part, 3)] + 1)
                for i in range(4):
                    u = unit_of[("A", c, part, i)]
                    for k in range(2):
                        kd = 2 * i + k
                        if part < 2:
                            lh, ll = hTh[:, kd, P * tb:P * tb + P], hTl[:, kd, P * tb:P * tb + P]
                        else:
                            lh, ll = value_tokens(hTh, kd, c % NA, tb), value_tokens(hTl, kd, c % NA, tb)
                        last = three(bank(t % 2), lh, ll, wview(u, False)[:, k, :], wview(u, True)[:, k, :],
                                     kd == 0, kd == KD - 1)
                    if tb == TB - 1 and i < 3:
                        last.then_inc(w_used, 1)
                last.then_inc(proj_done, 1)

            def transpose_qk(c, q):
                n = 2 * TB * c + q
                pe.wait_ge(rope_done, n + 1)
                if n >= 2:
                    pe.wait_ge(qkT_done, n - 1)
                if q < 2 and c:
                    pe.wait_ge(st_evac, c)
                for h in range(HALF):
                    last = nc.tensor.transpose(bank(2 + n % 2)[:, P * h:P * h + P],
                                               qn[:, n % 2, P * h:P * h + P], ident[:, :])
                last.then_inc(qt_done, 1)

            def scores(c, j):
                h, b, n = j // TB, j % TB, HALF * TB * c + j
                if j == 0:
                    pe.wait_ge(qkT_done, 2 * TB * (c + 1))
                if n >= 2:
                    pe.wait_ge(masked, n - 1)
                k0, kn = key_cols(c % NA, b)
                nc.tensor.matmul(bank(4 + n % 2)[:, 0:kn], qT[:, h, P * b:P * b + P], kT[:, h, k0:k0 + kn],
                                 start=True, stop=True).then_inc(s_done, 1)

            def transpose_p(c, j):
                n = HALF * TB * c + j
                pe.wait_ge(p_done, n + 1)
                if n >= 2:
                    pe.wait_ge(pt_ready, n - 1)
                for i in range(key_cols(c % NA, j % TB)[1] // P):
                    last = nc.tensor.transpose(bank(2 + n % 2)[:, P * i:P * i + P], pp[:, n % 2, P * i:P * i + P],
                                               ident[:, :])
                last.then_inc(ptr_done, 1)

            def values(c, j):
                h, b, n = j // TB, j % TB, HALF * TB * c + j
                if j == 0:
                    pe.wait_ge(v_done, TB * (c + 1))
                pe.wait_ge(pt_ready, n + 1)
                if n >= 8 and n % 4 == 0:
                    pe.wait_ge(u_evac, n // 4 - 1)
                vb = value_blocks(c % NA, b)
                for i, v in enumerate(vb):
                    last = nc.tensor.matmul(bank(6 + n // 4 % 2)[:, P * (n % 4):P * (n % 4) + P],
                                            vv[:, v, HD * h:HD * h + HD], pt[:, n % 2, P * i:P * i + P],
                                            start=(i == 0), stop=(i == len(vb) - 1))
                last.then_inc(pv_done, 1)

            for c in range(NCHUNK):
                for n in range(3 * TB):
                    project(c, n)
                    if 2 <= n < 2 * TB + 2:
                        transpose_qk(c, n - 2)
                for j in range(HALF * TB + 2):
                    if j < HALF * TB:
                        scores(c, j)
                    if 1 <= j <= HALF * TB:
                        transpose_p(c, j - 1)
                    if j >= 2:
                        values(c, j - 2)
                nc.tensor.transpose(bank(2)[0:2 * HALF * TB, 0:P], stat[:, :, :, :].rearrange("p s h b -> p (s h b)"),
                                    ident[:, :]).then_inc(stT_done, 1)

            for h in range(H):
                u = unit_of[("Y", h)]
                pe.wait_ge(w_lo, u + 1)
                if h < 4:
                    if h == 1:
                        pe.wait_ge(st_evac, NCHUNK)
                    if h == 3:
                        pe.wait_ge(u_evac, NCHUNK * HALF * TB // 4)
                else:
                    pe.wait_ge(ysilu_done, 2 * (h - 3))
                last = features_by_tokens(u, h % 4, KD, tok(hTh), tok(hTl))
                last.then_inc(yg_done, 1)
            for hf in range(2):
                for tb in range(TB):
                    n = hf * TB + tb
                    if tb == 0:
                        pe.wait_ge(w_lo, unit_of[("Z", hf, 3)] + 1)
                    if n == 0:
                        pe.wait_ge(y_done, 2 * H)
                        pe.wait_ge(ysilu_done, 2 * H)
                    if n >= 2:
                        pe.wait_ge(out_ready, n - 1)
                    for i in range(4):
                        u = unit_of[("Z", hf, i)]
                        for k in range(2):
                            hh = 2 * i + k
                            last = three(bank(n % 2), yh[:, hh, P * tb:P * tb + P], yl[:, hh, P * tb:P * tb + P],
                                         wview(u, False)[:, k, :], wview(u, True)[:, k, :], hh == 0, hh == H - 1)
                        if tb == TB - 1 and i < 3:
                            last.then_inc(w_used, 1)
                    last.then_inc(z1_done, 1)

        @block.vector
        def _(dve):
            steps = [0]

            def link(ins):
                steps[0] += 1
                ins.then_inc(dve_step, 1)
                dve.wait_ge(dve_step, steps[0])

            def inverse_root(v, s, t, y):
                link(nc.vector.reciprocal(y, s))
                link(nc.vector.tensor_tensor(t, y, y, ALU.mult))
                link(nc.vector.tensor_tensor(t, t, v, ALU.mult))
                link(nc.vector.tensor_scalar(t, t, -0.5, 1.5, ALU.mult, ALU.add))
                link(nc.vector.tensor_tensor(y, y, t, ALU.mult))

            def norm_x(layer):
                def lows(tb):
                    n = layer * TB + tb
                    dve.wait_ge(hhi_done, n + 1)
                    nc.vector.tensor_tensor(hTl[:, :, P * tb:P * tb + P],
                                            pair[tb % 2][:, :].rearrange("p (k c) -> p k c", k=KD),
                                            hTh[:, :, P * tb:P * tb + P].bitcast(F32), ALU.subtract).then_inc(hlo_done, 1)

                for tb in range(TB):
                    n = layer * TB + tb
                    if tb == 0:
                        dve.wait_ge(nw_in, 16 * (layer + 1))
                    dve.wait_ge(sq_done, n + 1)
                    nc.vector.tensor_scalar(var[:, tb:tb + 1], ss[:, tb:tb + 1], 1.0 / D, EPS, ALU.mult,
                                            ALU.add).then_inc(var_done, 1)
                    dve.wait_ge(root_done, n + 1)
                    c = slice(tb, tb + 1)
                    inverse_root(var[:, c], root[:, c], tmp[:, c], rstd[:, c])
                    buf = (bufU, bufS)[tb % 2]
                    nc.vector.scalar_tensor_tensor(out=buf[:, 0:D], in0=xs[:, tb, :], scalar=rstd[:, c],
                                                   in1=bufG[:, :], op0=ALU.mult, op1=ALU.mult).then_inc(xn_done, 1)
                    if tb >= 1:
                        lows(tb - 1)
                lows(TB - 1)
                if layer == 1:
                    dve.wait_ge(hlo_done, TB + 1)
                    nc.vector.tensor_copy(hTl[:, :, T:TPAD], hTl[:, :, 0:SIDE].bitcast(F32)).then_inc(hpad_done, 1)

            norm_x(0)
            dve.wait_ge(const_in, 16 * 3)

            def add_out(g, po):
                for tb in range(TB):
                    n = 2 * TB * g + TB * po + tb
                    dve.wait_ge(o_done, n + 1)
                    nc.vector.tensor_tensor(xs[:, tb, :], pair[pair_of[("O", g, po, tb)]][:, :], xs[:, tb, :],
                                            ALU.add).then_inc(o_added, 1)

            def pool_block(g, c):
                n = GB * g + c
                w = WINDOWS[g]
                dve.wait_ge(u_copied, n + 1)
                src, dst, k = bufU, bufS, 1
                while k < w:
                    ext = w // 2 - k
                    lo, num = PAD - ext, T + 2 * ext
                    s = max(k // 2, 1)
                    a, b = (-1, 0) if k == 1 else (-s, s)
                    link(nc.vector.tensor_tensor(dst[:, lo:lo + num], src[:, lo + a:lo + a + num],
                                                 src[:, lo + b:lo + b + num], ALU.add))
                    src, dst, k = dst, src, 2 * k
                ends = src[:, PAD:PAD + T].rearrange("p (a b) -> p a b", b=8)[:, 0:TB * 16:TB * 16 - 1, :]
                link(nc.vector.tensor_tensor(ends, ends, edge[:, g, :, :], ALU.mult))
                mid = src[:, PAD:PAD + T]
                nc.vector.scalar_tensor_tensor(out=mid, in0=mid, scalar=1.0 / w, in1=pair[pair_of[("U", g, c)]][:, :],
                                               op0=ALU.mult, op1=ALU.subtract).then_inc(d_ready, 1)
                dve.wait_ge(dhi_done, n + 1)
                nc.vector.tensor_tensor(diffl[:, c, :], mid, diffh[:, c, :].bitcast(F32),
                                        ALU.subtract).then_inc(diff_done, 1)
                if w >= 8:
                    link(nc.vector.memset(bufU[:, 0:PAD], 0.0))
                    link(nc.vector.memset(bufU[:, PAD + T:], 0.0))

            def z_block(g, c):
                n = GB * g + c
                dve.wait_ge(silu_done, n + 1)
                dve.wait_ge(m_done, n + 1)
                nc.vector.scalar_tensor_tensor(out=bufG[:, :], in0=pair[pair_of[("M", g, c)]][:, :],
                                               scalar=pscale[:, n:n + 1], in1=bufG[:, :], op0=ALU.mult,
                                               op1=ALU.mult).then_inc(z_ready, 1)
                dve.wait_ge(zhi_done, n + 1)
                nc.vector.tensor_tensor(zl[:, c % 2, :], bufG[:, :], zh[:, c % 2, :].bitcast(F32),
                                        ALU.subtract).then_inc(z_done, 1)

            dve.wait_ge(xt_done, TB)
            link(nc.vector.memset(bufU[:, 0:PAD], 0.0))
            link(nc.vector.memset(bufU[:, PAD + T:], 0.0))
            for g in range(NG):
                pool_block(g, 0)
                if g:
                    add_out(g - 1, 1)
                for c in range(1, GB):
                    pool_block(g, c)
                z_block(g, 0)
                z_block(g, 1)
                add_out(g, 0)
                z_block(g, 2)
                z_block(g, 3)
            add_out(NG - 1, 1)

            norm_x(1)
            dve.wait_ge(x1_out, 16 * TB)
            dve.wait_ge(acon_in, 16 * 9)
            nc.vector.memset(kT[:, :, 0:SIDE], 0.0).then_inc(kpad_set, 1)
            nc.vector.memset(kT[:, :, SIDE + T:], 0.0).then_inc(kpad_set, 1)
            nc.vector.memset(wcol[0:ROPE, :], 1.0).then_inc(wcol_set, 1)

            def fold(g, part):
                i = 2 * g + part
                hr = ROPE // 2
                w = wrow[:, i, :].unsqueeze(1)
                nc.vector.tensor_tensor(cosw[:, :, :], cosb[:, :, :], w.to_broadcast([P, TB, ROPE]), ALU.mult)
                nc.vector.tensor_tensor(sinw[:, :, 0:hr], sinb[:, :, 0:hr],
                                        w[:, :, hr:].to_broadcast([P, TB, hr]), ALU.mult)
                link(nc.vector.tensor_tensor(sinw[:, :, hr:], sinb[:, :, hr:],
                                             w[:, :, 0:hr].to_broadcast([P, TB, hr]), ALU.mult))

            def norm_rotate(c, q):
                n = 2 * TB * c + q
                tb, t = q % TB, 3 * TB * c + q
                x4 = qn[:, n % 2, :].rearrange("p (h e) -> p h e", h=HALF)
                dve.wait_ge(qsq_done, n + 1)
                link(nc.vector.tensor_reduce(qss[:, :], x4, AX_X, ALU.add))
                nc.vector.tensor_scalar(qvar[:, :], qss[:, :], 1.0 / HD, EPS, ALU.mult, ALU.add).then_inc(qvar_done, 1)
                dve.wait_ge(qroot_done, n + 1)
                inverse_root(qvar[:, :], qroot[:, :], qtmp[:, :], qrstd[:, :])
                nc.vector.tensor_tensor(x4, bank(t % 2).rearrange("p (h e) -> p h e", h=HALF),
                                        qrstd[:, :].unsqueeze(2).to_broadcast([P, HALF, HD]),
                                        ALU.mult).then_inc(qn_done, 1)
                dve.wait_ge(qn_done, n + 1)
                hr = ROPE // 2
                cw, sw = cosw[:, tb, :].unsqueeze(1), sinw[:, tb, :].unsqueeze(1)
                nc.vector.tensor_tensor(ropeA[:, :, :], x4[:, :, 0:ROPE], cw.to_broadcast([P, HALF, ROPE]), ALU.mult)
                nc.vector.tensor_tensor(ropeB[:, :, 0:hr], x4[:, :, hr:ROPE],
                                        sw[:, :, 0:hr].to_broadcast([P, HALF, hr]), ALU.mult)
                link(nc.vector.tensor_tensor(ropeB[:, :, hr:], x4[:, :, 0:hr],
                                             sw[:, :, hr:].to_broadcast([P, HALF, hr]), ALU.mult))
                nc.vector.tensor_tensor(x4[:, :, 0:ROPE], ropeA[:, :, :], ropeB[:, :, :], ALU.add).then_inc(rope_done, 1)

            def row_max(c, j):
                n, b = HALF * TB * c + j, j % TB
                g = c % NA
                kn = key_cols(g, b)[1]
                dve.wait_ge(s_done, n + 1)
                if n >= 2:
                    dve.wait_ge(ptr_done, n - 1)
                if j == 0 and c:
                    dve.wait_ge(stT_done, c)
                if n >= 2:
                    dve.wait_ge(p_done, n - 1)
                nc.vector.tensor_tensor_reduce(pp[:, n % 2, 0:kn], bank(4 + n % 2)[:, 0:kn], mask_of(g, b), 1.0, -3e38,
                                               ALU.add, ALU.max, mmax[:, n % 2:n % 2 + 1]).then_inc(masked, 1)
                dve.wait_ge(masked, n + 1)
                h = j // TB
                nc.vector.tensor_scalar(stat[:, 0, h, b:b + 1], mmax[:, n % 2:n % 2 + 1], -SCALE, None,
                                        ALU.mult).then_inc(m_ready, 1)

            def take_pt(c, j):
                n = HALF * TB * c + j
                kn = key_cols(c % NA, j % TB)[1]
                dve.wait_ge(ptr_done, n + 1)
                if n >= 2:
                    dve.wait_ge(pv_done, n - 1)
                nc.vector.tensor_copy(pt[:, n % 2, 0:kn], bank(2 + n % 2)[:, 0:kn]).then_inc(pt_ready, 1)

            for c in range(NCHUNK):
                for q in range(2 * TB):
                    if q % TB == 0:
                        fold(c % NA, q // TB)
                    norm_rotate(c, q)
                for j in range(HALF * TB + 1):
                    if j < HALF * TB:
                        row_max(c, j)
                    if j >= 1:
                        take_pt(c, j - 1)

            dve.wait_ge(f_in, 16 * 2 * NA * H)

            def grouped(t, g):
                if g == 0:
                    return t[:, g, :]
                return t[:, g, :].rearrange("p (r j) -> p j r", r=STRIDE[g])

            def natural(t2, g):
                return t2 if g == 0 else t2.rearrange("p (j r) -> p j r", r=STRIDE[g])

            link(nc.vector.tensor_copy(ftot[:, :], fm[:, 0, :]))
            for g in (1, 2):
                link(nc.vector.tensor_tensor(natural(ftot[:, :], g), natural(ftot[:, :], g), grouped(fm, g), ALU.min))
            for g in range(NA):
                op = nc.vector.tensor_tensor(grouped(fm, g), natural(ftot[:, :], g), grouped(fm, g), ALU.subtract)
                link(op)
            nc.vector.memset(ftot[:, :], 0.0).then_inc(f_sub, 1)
            dve.wait_ge(f_exp, 1)
            dve.wait_ge(f_sub, 1)
            for g in range(NA):
                link(nc.vector.tensor_tensor(fden[:, g, :], fden[:, g, :], fm[:, g, :], ALU.mult))
                link(nc.vector.tensor_tensor(natural(ftot[:, :], g), natural(ftot[:, :], g), grouped(fden, g), ALU.add))
            link(nc.vector.reciprocal(ftot[:, :], ftot[:, :]))
            for g in range(NA):
                last = nc.vector.tensor_tensor(natural(fden[:, g, :], g), grouped(fm, g), natural(ftot[:, :], g),
                                               ALU.mult)
            last.then_inc(f_ready, 1)

            for i in range(2 * H):
                h, hf = i // 2, i % 2
                dve.wait_ge(uf_in, 16 * 6 * (i + 1))
                for g in range(NA):
                    op = nc.vector.tensor_tensor(uf[:, g, :], uf[:, g, :], uf[:, NA + g, :], ALU.mult)
                link(op)
                link(nc.vector.tensor_tensor(uf[:, 0, :], uf[:, 0, :], uf[:, 1, :], ALU.add))
                link(nc.vector.tensor_tensor(uf[:, 0, :], uf[:, 0, :], uf[:, 2, :], ALU.add))
                dve.wait_ge(ysilu_done, i + 1)
                nc.vector.tensor_tensor(gate[:, :], uf[:, 0, :], gate[:, :], ALU.mult).then_inc(y_ready, 1)
                dve.wait_ge(yhi_done, i + 1)
                nc.vector.tensor_tensor(yl[:, h, 512 * hf:512 * hf + 512], gate[:, :],
                                        yh[:, h, 512 * hf:512 * hf + 512].bitcast(F32), ALU.subtract).then_inc(y_done, 1)

            for n in range(2 * TB):
                dve.wait_ge(x1_in[n % 3], 16 * (n // 3 + 1))
                dve.wait_ge(z1_done, n + 1)
                s = n % 3
                nc.vector.tensor_tensor(uf[:, s, :], bank(n % 2), uf[:, s, :], ALU.add).then_inc(out_ready, 1)

        @block.scalar
        def _(act):
            steps = [0]
            for tb in range(TB):
                act.dma_start(xs[:, tb, :], x2[P * tb:P * tb + P, :]).then_inc(xin[tb], 16)
            act.dma_start(bufG[:, :], pool_norm[0:1, :].to_broadcast([P, D])).then_inc(nw_in, 16)
            act.dma_start(ident[:, :], ident_d).then_inc(const_in, 16)
            act.dma_start(pscale[:, :], pool_scale[0].rearrange("(c p) -> p c", p=P),
                          allow_slow_non_contiguous=True).then_inc(const_in, 16)
            act.dma_start(edge[:, :, :, :].rearrange("p g a b -> p (g a b)"),
                          edge_d.to_broadcast([P, NG * 16])).then_inc(const_in, 16)

            def norm_x(layer):
                def highs(tb):
                    n = layer * TB + tb
                    act.wait_ge(xt_done, n + 1)
                    nc.scalar.activation(hTh[:, :, P * tb:P * tb + P],
                                         pair[tb % 2][:, :].rearrange("p (k c) -> p k c", k=KD),
                                         ACT.Copy).then_inc(hhi_done, 1)

                for tb in range(TB):
                    n = layer * TB + tb
                    if layer == 0:
                        act.wait_ge(xin[tb], 16)
                    else:
                        act.wait_ge(o_added, 2 * TB * NG - TB + tb + 1)
                        act.dma_start(x1_d[P * tb:P * tb + P, :], xs[:, tb, :]).then_inc(x1_out, 16)
                    if tb >= 2:
                        act.wait_ge(xt_done, n - 1)
                    buf = (bufU, bufS)[tb % 2]
                    nc.scalar.activation(buf[:, 0:D], xs[:, tb, :], ACT.Square,
                                         accum_out=ss[:, tb:tb + 1]).then_inc(sq_done, 1)
                    act.wait_ge(var_done, n + 1)
                    nc.scalar.activation(root[:, tb:tb + 1], var[:, tb:tb + 1], ACT.Sqrt).then_inc(root_done, 1)
                    if tb >= 1:
                        highs(tb - 1)
                highs(TB - 1)
                if layer == 1:
                    act.wait_ge(hhi_done, TB + 1)
                    nc.scalar.activation(hTh[:, :, T:TPAD], hTh[:, :, 0:SIDE].bitcast(F32),
                                         ACT.Copy).then_inc(hpad_done, 1)

            norm_x(0)
            for g in range(NG):
                for c in range(GB):
                    n = GB * g + c
                    act.wait_ge(u_done, n + 1)
                    if n == 0:
                        act.wait_ge(xt_done, TB)
                    else:
                        act.wait_ge(diff_done, n)
                    nc.scalar.activation(bufU[:, PAD:PAD + T], pair[pair_of[("U", g, c)]][:, :],
                                         ACT.Copy).then_inc(u_copied, 1)
                    act.wait_ge(d_ready, n + 1)
                    if g:
                        act.wait_ge(m_done, GB * g)
                    fin = bufU if g % 2 else bufS
                    nc.scalar.activation(diffh[:, c, :], fin[:, PAD:PAD + T], ACT.Copy).then_inc(dhi_done, 1)
                for c in range(GB):
                    n = GB * g + c
                    act.wait_ge(g_done, n + 1)
                    if n == 0:
                        act.wait_ge(xn_done, TB)
                    else:
                        act.wait_ge(z_done, n)
                    nc.scalar.activation(bufG[:, :], pair[pair_of[("G", g, c)]][:, :], ACT.Silu).then_inc(silu_done, 1)
                    act.wait_ge(z_ready, n + 1)
                    if n >= 2:
                        act.wait_ge(o_done, 2 * TB * ((n - 2) // GB) + TB * ((n - 2) % GB // 2) + TB)
                    nc.scalar.activation(zh[:, c % 2, :], bufG[:, :], ACT.Copy).then_inc(zhi_done, 1)

            act.wait_ge(z_done, GB * NG)
            act.dma_start(bufG[:, :], att_norm[0:1, :].to_broadcast([P, D])).then_inc(nw_in, 16)
            norm_x(1)
            act.wait_ge(hlo_done, 2 * TB)
            act.wait_ge(x1_out, 16 * TB)
            act.dma_start(mask0[:, :, :], mask0_d.rearrange("m p c -> p m c")).then_inc(acon_in, 16)
            act.dma_start(mask1[:, :, :], mask1_d.rearrange("m p c -> p m c")).then_inc(acon_in, 16)
            act.dma_start(mask2[:, :], mask2_d).then_inc(acon_in, 16)
            act.dma_start(cosb[:, :, :], cos_d.rearrange("(b p) e -> p b e", p=P)).then_inc(acon_in, 16)
            act.dma_start(sinb[:, :, :], sin_d.rearrange("(b p) e -> p b e", p=P)).then_inc(acon_in, 16)
            wr = wrow[:, :, :].rearrange("p (g k) e -> p k g e", k=2)
            wc = wcol[ROPE:P, :].rearrange("p (g k) -> p k g", k=2)
            for k, w in enumerate((att_q_norm, att_k_norm)):
                act.dma_start(wr[:, k], w[0:1, :, 0:ROPE].to_broadcast([P, NA, ROPE])).then_inc(acon_in, 16)
                act.dma_start(wc[:, k], w[0, :, ROPE:HD].rearrange("g e -> e g"),
                              allow_slow_non_contiguous=True).then_inc(acon_in, 16)
            act.wait_ge(acon_in, 16 * 9)
            act.wait_ge(wcol_set, 1)
            act.wait_ge(kpad_set, 2)

            def square(c, q):
                n, t = 2 * TB * c + q, 3 * TB * c + q
                act.wait_ge(proj_done, t + 1)
                if n >= 2:
                    act.wait_ge(qt_done, n - 1)
                nc.scalar.activation(qn[:, n % 2, :], bank(t % 2), ACT.Square).then_inc(qsq_done, 1)

            def root_q(c, q):
                n = 2 * TB * c + q
                act.wait_ge(qvar_done, n + 1)
                nc.scalar.activation(qroot[:, :], qvar[:, :], ACT.Sqrt).then_inc(qroot_done, 1)

            def take_qk(c, q):
                n, g = 2 * TB * c + q, c % NA
                part, tb = q // TB, q % TB
                act.wait_ge(qt_done, n + 1)
                src = bank(2 + n % 2).rearrange("p (h t) -> p h t", h=HALF)
                dst = qT[:, :, :] if part == 0 else kT[:, :, SIDE:SIDE + T]
                if q % TB == 0 and c:
                    act.wait_ge(s_done, HALF * TB * c)
                if g == 0:
                    dst = dst[:, :, P * tb:P * tb + P]
                else:
                    dil = STRIDE[g]
                    m = P // dil
                    src = src.rearrange("p h (j r) -> p h r j", r=dil)
                    dst = dst.rearrange("p h (r s) -> p h r s", r=dil)[:, :, :, m * tb:m * tb + m]
                i = 2 * g + part
                nc.scalar.activation(dst, src, ACT.Copy, scale=wcol[:, i:i + 1]).then_inc(qkT_done, 1)

            def take_v(c, b):
                act.wait_ge(proj_done, 3 * TB * c + 2 * TB + b + 1)
                if b == 0 and c:
                    act.wait_ge(pv_done, HALF * TB * c)
                nc.scalar.activation(vv[:, b, :], bank((3 * TB * c + 2 * TB + b) % 2), ACT.Copy).then_inc(v_done, 1)

            def exps(c, j):
                n = HALF * TB * c + j
                h, b = j // TB, j % TB
                kn = key_cols(c % NA, b)[1]
                act.wait_ge(m_ready, n + 1)
                nc.scalar.activation(pp[:, n % 2, 0:kn], pp[:, n % 2, 0:kn], ACT.Exp, bias=stat[:, 0, h, b:b + 1],
                                     scale=SCALE, accum_out=stat[:, 1, h, b:b + 1]).then_inc(p_done, 1)

            def take_u(c, i):
                n, g, h = HALF * TB // 4 * c + i, c % NA, i // 2
                act.wait_ge(pv_done, 4 * (n + 1))
                if i % 2 == 0 and n:
                    act.wait_ge(u_out, 16 * (n // 2))
                src = bank(6 + n % 2)
                half = i % 2
                if g == 0:
                    dst = uo[:, 512 * half:512 * half + 512]
                else:
                    dil = STRIDE[g]
                    m = dil // 2
                    src = src.rearrange("p (r s) -> p r s", r=m)
                    dst = uo[:, :].rearrange("p (s r) -> p r s", r=dil)[:, m * half:m * half + m, :]
                nc.scalar.activation(dst, src, ACT.Copy).then_inc(u_evac, 1)
                if half:
                    act.wait_ge(u_evac, n + 1)
                    act.dma_start(u_d[g, HALF * (c // NA) + h], uo[:, :]).then_inc(u_out, 16)

            for c in range(NCHUNK):
                for n in range(3 * TB):
                    if n < 2 * TB:
                        square(c, n)
                    if 2 <= n < 2 * TB + 2:
                        take_qk(c, n - 2)
                    if n < 2 * TB:
                        root_q(c, n)
                    else:
                        take_v(c, n - 2 * TB)
                for j in range(HALF * TB):
                    if j == 0 and c:
                        act.wait_ge(stT_done, c)
                    exps(c, j)
                    if j % 4 == 3 and j > 4:
                        take_u(c, j // 4 - 1)
                take_u(c, HALF * TB // 4 - 1)
                act.wait_ge(stT_done, c + 1)
                if c:
                    act.wait_ge(st_out, 16 * c)
                nc.scalar.activation(statT[:, :], bank(2)[0:2 * HALF * TB, 0:P], ACT.Copy).then_inc(st_evac, 1)
                act.wait_ge(st_evac, c + 1)
                half, g = c // NA, c % NA
                dst = st_d[g, :, HALF * half:HALF * half + HALF, :].rearrange("s h (b q) -> s h b q", q=P)
                for s in range(2):
                    act.dma_start(dst[s].rearrange("h b q -> (h b) q"),
                                  statT[s * HALF * TB:(s + 1) * HALF * TB, :]).then_inc(st_out, 8 * 1 if False else 16)

            act.wait_ge(st_out, 16 * 2 * NCHUNK)
            act.wait_ge(u_out, 16 * NA * H)
            for g in range(NA):
                dil = STRIDE[g]
                for s, t in enumerate((fm, fden)):
                    for h in range(H):
                        if g == 0:
                            src = st_d[g, s, h].rearrange("(t q) -> t q", t=TB)
                            dst = t[TB * h:TB * h + TB, g, :]
                        else:
                            src = st_d[g, s, h].rearrange("(r t j) -> t r j", r=dil, t=TB)
                            dst = t[TB * h:TB * h + TB, g, :].rearrange("p (r j) -> p r j", r=dil)
                        act.dma_start(dst, src).then_inc(f_in, 16)
            act.wait_ge(f_sub, 1)
            nc.scalar.activation(fm[:, :, :], fm[:, :, :], ACT.Exp).then_inc(f_exp, 1)
            act.wait_ge(f_ready, 1)
            for g in range(NA):
                act.dma_start(f_d[g].rearrange("h (t q) -> (h t) q", q=P), fden[:, g, :]).then_inc(f_out, 16)
            act.wait_ge(f_out, 16 * NA)

            def load_merge(i):
                h, hf = i // 2, i % 2
                if i:
                    act.wait_ge(y_ready, i)
                for g in range(NA):
                    act.dma_start(uf[:, g, :], u_d[g, h][:, 512 * hf:512 * hf + 512]).then_inc(uf_in, 16)
                    act.dma_start(uf[:, NA + g, :],
                                  f_d[g, h:h + 1, 512 * hf:512 * hf + 512].to_broadcast([P, 512])).then_inc(uf_in, 16)

            load_merge(0)
            for i in range(2 * H):
                h, hf = i // 2, i % 2
                act.wait_ge(yg_done, h + 1)
                if i:
                    act.wait_ge(y_done, i)
                nc.scalar.activation(gate[:, :], pair[h % 4][:, 512 * hf:512 * hf + 512], ACT.Silu).then_inc(ysilu_done, 1)
                act.wait_ge(y_ready, i + 1)
                nc.scalar.activation(yh[:, h, 512 * hf:512 * hf + 512], gate[:, :], ACT.Copy).then_inc(yhi_done, 1)
                if i + 1 < 2 * H:
                    load_merge(i + 1)

            def tile(t, n):
                hf, tb = n // TB, n % TB
                return t[P * tb:P * tb + P, 512 * hf:512 * hf + 512]

            act.wait_ge(y_done, 2 * H)
            for n in range(2 * TB + 1):
                if n < 2 * TB:
                    if n >= 3:
                        act.wait_ge(out_sent[n % 3], 16 * (n // 3))
                    act.dma_start(uf[:, n % 3, :], tile(x1_d, n)).then_inc(x1_in[n % 3], 16)
                if n >= 1:
                    act.wait_ge(out_ready, n)
                    act.dma_start(tile(out2, n - 1), uf[:, (n - 1) % 3, :]).then_inc(out_sent[(n - 1) % 3], 16)
            for i in range(3):
                act.wait_ge(out_sent[i], 16 * len(range(i, 2 * TB, 3)))


_INS = ["x", "pool_norm", "pool_w_in", "pool_w_group", "pool_scale", "pool_w_out", "att_norm", "att_w_in",
        "att_q_norm", "att_k_norm", "att_w_out"]


def shape_constants(T):
    import numpy as np
    neg = np.float32(-1e30)
    ident = np.eye(P, dtype=np.float32)
    q, c = np.arange(P)[:, None], np.arange(256)[None, :]
    band = (c - q >= 0) & (c - q <= 2 * SIDE)
    ok0 = np.stack([band & (c >= SIDE), band, band & (c < 256 - SIDE)])
    ok1 = np.stack([np.abs(c - (P * b + q)) <= SIDE for b in range(2)])
    ok2 = (q % 2) == (c[:, :P] % 2)
    masks = [np.where(m, np.float32(0), neg).astype(np.float32) for m in (ok0, ok1, ok2)]
    half = ROPE // 2
    f32 = np.float32
    inv = (f32(1.0) / (f32(500000.0) ** (np.arange(half, dtype=f32) * f32(2.0) / f32(ROPE)))).astype(f32)
    ang = np.arange(T, dtype=f32)[:, None] * inv[None, :]
    cos, sin = np.cos(ang).astype(f32), np.sin(ang).astype(f32)
    edge = np.ones((len(WINDOWS), 2, 8), f32)
    for g, w in enumerate(WINDOWS):
        for i, t in enumerate(list(range(8)) + list(range(T - 8, T))):
            n = min(t - w // 2 + w, T) - max(t - w // 2, 0)
            edge[g, i // 8, i % 8] = f32(w / n)
    return {"ident": ident, "mask0": masks[0], "mask1": masks[1], "mask2": masks[2],
            "cos": np.concatenate([cos, cos], 1), "sin": np.concatenate([-sin, sin], 1),
            "edge": edge.reshape(1, -1)}


def kernel(**inputs):
    import numpy as np
    import concourse.bacc as bacc
    from concourse.bass_utils import run_bass_kernel_spmd as run

    nc = bacc.Bacc("TRN2", target_bir_lowering=False, num_devices=1)
    arrays, args = {}, []
    given = {n: np.ascontiguousarray(inputs[n]) for n in _INS}
    given.update(shape_constants(inputs["x"].shape[1]))
    for name, a in given.items():
        arrays[f"in_{name}_dram"] = a
        args.append(nc.dram_tensor(f"in_{name}_dram", a.shape, mybir.dt.from_np(a.dtype), kind="ExternalInput").ap())
    shape = inputs["x"].shape
    args.append(nc.dram_tensor("out_dram", shape, F32, kind="ExternalOutput").ap())
    encoder_program(nc, *args)
    r = run(nc, [arrays], core_ids=[0])
    return r.results[0]["out_dram"]
```

```python
from contextlib import ExitStack

import concourse.bass as bass
from concourse import mybir

F32 = mybir.dt.float32
F32R = mybir.dt.float32r
I32 = mybir.dt.int32
ALU = mybir.AluOpType
ACT = mybir.ActivationFunctionType
AX_X = mybir.AxisListType.X

P = 128
EPS = 1e-6
ROPE = 32
SIDE = 64
STRIDE = (1, 4, 8)
WINDOWS = (2, 4, 8, 16)
PAD = 8


def encoder_program(nc, x, pool_norm, pool_w_in, pool_w_group, pool_scale, pool_w_out, att_norm, att_w_in,
                    att_q_norm, att_k_norm, att_w_out, ident_d, mask0_d, mask1_d, mask2_d, cos_d, sin_d,
                    edge_d, out):
    T, D = x.shape[1], x.shape[2]
    TB, KD = T // P, D // P
    PW = pool_w_out.shape[1]
    NG = len(WINDOWS)
    GB = PW // NG // P
    HD = P
    H = D // HD
    NA = len(STRIDE)
    HALF = 4
    SCALE = float(HD) ** -0.5
    TPAD = T + SIDE
    KW = T + 2 * SIDE
    NCHUNK = (H // HALF) * NA
    Q, K, V = range(3)
    PARTS = (K, V, Q)

    x2 = x[0]
    out2 = out[0]
    w_in0, w_out0 = pool_w_in[0], pool_w_out[0]
    w_in1, w_out1 = att_w_in[0], att_w_out[0]

    x1_d = nc.dram_tensor("x1_spill", (T, D), F32, kind="Internal").ap()
    u_d = nc.dram_tensor("u_spill", (NA, H, P, T), F32, kind="Internal").ap()
    st_d = nc.dram_tensor("stat_spill", (NA, 2, H, T), F32, kind="Internal").ap()
    o_d = nc.dram_tensor("merged_spill", (H, P, T), F32, kind="Internal").ap()
    f_d = nc.dram_tensor("factor_spill", (NA, H, T), F32, kind="Internal").ap()

    def cols(w, j, n, k0, k):
        return w[k0 * P:(k0 + k) * P, j:j + n].rearrange("(k p) c -> p k c", p=P)

    units = []
    unit_of = {}

    def add(key, src, k, n):
        unit_of[key] = len(units)
        units.append((src, k, n))

    for g in range(NG):
        def wout_units(gg, pair):
            for i in range(2):
                add(("O", gg, pair, i), cols(w_out0, 0, D, gg * GB + 2 * pair + i, 1), 1, D)

        def wgroup_unit(pair):
            add(("M", g, pair), cols(pool_w_group[0, g], 256 * pair, 256, 0, GB), GB, 256)

        def win_unit(kind, c):
            add((kind, g, c), cols(w_in0, (g * GB + c) * P + (PW if kind == "G" else 0), P, 0, KD), KD, P)

        win_unit("U", 0)
        if g:
            wout_units(g - 1, 1)
        for c in range(1, GB):
            win_unit("U", c)
        win_unit("G", 0)
        wgroup_unit(0)
        win_unit("G", 1)
        win_unit("G", 2)
        wout_units(g, 0)
        wgroup_unit(1)
        win_unit("G", 3)
    wout_units(NG - 1, 1)
    UNITS0 = len(units)
    for half in range(H // HALF):
        for g in range(NA):
            for part in PARTS:
                base = (g * 3 + part) * D + half * HALF * HD
                for i in range(4):
                    add(("A", half * NA + g, part, i), cols(w_in1, base, HALF * HD, 2 * i, 2), 2, HALF * HD)
    for h in range(H):
        add(("Y", h), cols(w_in1, 3 * NA * D + h * HD, P, 0, KD), KD, P)
    for hf in range(2):
        for i in range(4):
            add(("Z", hf, i), cols(w_out1, hf * 512, 512, 2 * i, 2), 2, 512)
    NU = len(units)
    R0, R1, RAW = 4, 6, 2

    def slot(u):
        return u % R0 if u < UNITS0 else (u - UNITS0) % R1

    ctx = ExitStack()
    with ctx:
        def sb(name, shape, dt, stack=ctx):
            return stack.enter_context(nc.sbuf_tensor(name, shape, dt))

        sems = {}

        def sem(name):
            if name not in sems:
                sems[name] = ctx.enter_context(nc.semaphore(name))
            return sems[name]

        hTh = sb("hTh", [P, KD, TPAD], F32R)
        hTl = sb("hTl", [P, KD, TPAD], F32R)
        raw = sb("raw", [P, RAW, 1024], F32)
        ident = sb("ident", [P, P], F32)
        zero = sb("zero", [P, 1], F32)
        edge = sb("edge", [P, NG, 2, 8], F32)
        pscale = sb("pscale", [P, PW // P], F32)
        ss = sb("ss", [P, TB], F32)
        var = sb("var", [P, TB], F32)
        tmp = sb("tmp", [P, TB], F32)
        rstd = sb("rstd", [P, TB], F32)
        with ExitStack() as l0:
            diff = sb("diff", [P, 2, GB, T], F32R, l0)
            diffh, diffl = diff[:, 0], diff[:, 1]
            w0 = sb("w0", [P, R0, 2, 1024], F32R, l0)
            zh = sb("zh", [P, 2, T], F32R, l0)
            zl = sb("zl", [P, 2, T], F32R, l0)
            xs = sb("xs", [P, TB, D], F32, l0)
            bufU = sb("bufU", [P, T + 2 * PAD], F32, l0)
            bufS = sb("bufS", [P, T + 2 * PAD], F32, l0)
            bufG = sb("bufG", [P, T], F32, l0)
        with ExitStack() as l1:
            w1 = sb("w1", [P, R1, 2, 1024], F32R, l1)
            uf = sb("uf", [P, 6, 512], F32, l1)
            with ExitStack() as la:
                qn = sb("qn", [P, 2, HALF * HD], F32, la)
                mask0 = sb("mask0", [P, 3, 256], F32, la)
                mask1 = sb("mask1", [P, 2, 256], F32, la)
                mask2 = sb("mask2", [P, P], F32, la)
                cosb = sb("cosb", [P, NA, TB, ROPE], F32, la)
                sinb = sb("sinb", [P, NA, TB, ROPE], F32, la)
                cosw = sb("cosw", [P, TB, ROPE], F32, la)
                sinw = sb("sinw", [P, TB, ROPE], F32, la)
                wrow = sb("wrow", [P, 2 * NA, ROPE], F32, la)
                wcol = sb("wcol", [P, 2 * NA], F32, la)
                ropeA = sb("ropeA", [P, HALF, ROPE], F32, la)
                ropeB = sb("ropeB", [P, HALF, ROPE], F32, la)
                qss = sb("qss", [P, HALF], F32, la)
                qvar = sb("qvar", [P, HALF], F32, la)
                qtmp = sb("qtmp", [P, HALF], F32, la)
                qrstd = sb("qrstd", [P, HALF], F32, la)
                qT = sb("qT", [P, 2, HALF, P], F32, la)
                kT = sb("kT", [P, HALF, KW], F32, la)
                vv = sb("vv", [P, TB, HALF * HD], F32, la)
                uo = sb("uo", [P, 2, HALF, P], F32, la)
                pp = sb("pp", [P, 2, 256], F32, la)
                pt = sb("pt", [P, 2, 256], F32, la)
                stat = sb("stat", [P, 2, HALF, TB], F32, la)
                statT = sb("statT", [2 * HALF * TB, P], F32, la)
            with ExitStack() as ly:
                yh = sb("yh", [P, H, T], F32R, ly)
                yl = sb("yl", [P, H, T], F32R, ly)
                yo = sb("yo", [P, 2, 512], F32, ly)
            with ExitStack() as ly:
                gate = sb("gate", [P, H, T], F32, ly)
                mixed = sb("mixed", [P, H, T], F32, ly)
            fm = uf[0:HALF * TB, NA, 0:NA * P].rearrange("p (g c) -> p g c", g=NA)
            fden = uf[0:HALF * TB, NA + 1, 0:NA * P].rearrange("p (g c) -> p g c", g=NA)
            ftot = uf[0:HALF * TB, NA + 2, 0:P]
            uf2 = gate[:, H - 3:H, :].rearrange("p a (b c) -> p (a b) c", b=2)

        pair = [ctx.enter_context(nc.psum_tensor(f"pair{i}", [P, 1024], F32)) for i in range(4)]

        def bank(i):
            return pair[i // 2][:, 512 * (i % 2):512 * (i % 2) + 512]

        def wview(u, lo):
            src, k, n = units[u]
            t = w0 if u < UNITS0 else w1
            return t[:, slot(u), 1 if lo else 0, :].rearrange("p (k c) -> p k c", k=k)

        xin = [sem(f"xin{i}") for i in range(TB)]
        raw_in = [sem(f"raw_in{i}") for i in range(RAW)]
        w_hi, w_lo, w_used = sem("w_hi"), sem("w_lo"), sem("w_used")
        const_in, zero_set = sem("const_in"), sem("zero_set")
        nw_in = sem("nw_in")
        sq_done, xn_done = sem("sq_done"), sem("xn_done")
        xt_done, hhi_done, hlo_done, hpad_done = sem("xt_done"), sem("hhi_done"), sem("hlo_done"), sem("hpad_done")
        u_done, g_done, m_done, o_done = sem("u_done"), sem("g_done"), sem("m_done"), sem("o_done")
        u_copied, d_ready, dhi_done, diff_done = sem("u_copied"), sem("d_ready"), sem("dhi_done"), sem("diff_done")
        silu_done, z_ready, zhi_done, z_done, o_added = (sem("silu_done"), sem("z_ready"), sem("zhi_done"),
                                                         sem("z_done"), sem("o_added"))
        x1_out = sem("x1_out")
        acon_in, kpad_set, wcol_set = sem("acon_in"), sem("kpad_set"), sem("wcol_set")
        proj_done, qsq_done = sem("proj_done"), sem("qsq_done")
        qn_done, rope_done, qt_done, qkT_done, v_done = (sem("qn_done"), sem("rope_done"), sem("qt_done"),
                                                         sem("qkT_done"), sem("v_done"))
        s_done, masked, p_done, ptr_done, pt_ready, pv_done, u_evac = (
            sem("s_done"), sem("masked"), sem("p_done"), sem("ptr_done"), sem("pt_ready"), sem("pv_done"),
            sem("u_evac"))
        u_out = [sem("u_out0"), sem("u_out1")]
        stT_done, st_evac, st_out = sem("stT_done"), sem("st_evac"), sem("st_out")
        f_in, f_sub, f_exp, f_ready, f_out = sem("f_in"), sem("f_sub"), sem("f_exp"), sem("f_ready"), sem("f_out")
        uf_in, merged, o_out = [sem("uf_in0"), sem("uf_in1")], sem("merged"), sem("o_out")
        o_in = [sem(f"o_in{i}") for i in range(HALF)]
        yg_done, ysilu_done, y_ready, yhi_done, y_done = (sem("yg_done"), sem("ysilu_done"), sem("y_ready"),
                                                          sem("yhi_done"), sem("y_done"))
        z1_done, out_ready = sem("z1_done"), sem("out_ready")
        x1_in = [sem(f"x1_in{i}") for i in range(3)]
        out_sent = [sem(f"out_sent{i}") for i in range(3)]
        dve_step, act_step, pool_step = sem("dve_step"), sem("act_step"), sem("pool_step")

        jobs = []
        for g in range(NG):
            jobs.append(("U", g, 0))
            if g:
                jobs += [("O", g - 1, 1, tb) for tb in range(TB)]
            jobs += [("U", g, c) for c in range(1, GB)]
            jobs += [("G", g, 0), ("M", g, 0), ("G", g, 1), ("M", g, 1), ("G", g, 2)]
            jobs += [("O", g, 0, tb) for tb in range(TB)]
            jobs += [("M", g, 2), ("G", g, 3), ("M", g, 3)]
        jobs += [("O", NG - 1, 1, tb) for tb in range(TB)]
        pair_of = {j: n % 4 for n, j in enumerate(jobs)}
        for n, j in enumerate(jobs[-TB:]):
            pair_of[j] = n % 3
        users = [None] * 4
        before = {}
        for j in jobs:
            before[j] = users[pair_of[j]]
            users[pair_of[j]] = j
        before["x"] = users[3]

        def released(job):
            kind, g = job[0], job[1]
            if kind == "U":
                return d_ready, GB * g + job[2] + 1
            if kind == "G":
                return silu_done, GB * g + job[2] + 1
            if kind == "M":
                return z_ready, GB * g + job[2] + 1
            return o_added, 2 * TB * g + TB * job[2] + job[3] + 1

        key_of = {n: key for key, n in unit_of.items()}

        def unit_released(u):
            key = key_of[u]
            kind, g = key[0], key[1]
            if kind == "U":
                return u_done, GB * g + key[2] + 1
            if kind == "G":
                return g_done, GB * g + key[2] + 1
            if kind == "M":
                return m_done, GB * g + 2 * key[2] + 2
            if kind == "O":
                return o_done, 2 * TB * g + TB * key[2] + TB
            if kind == "Y":
                return yg_done, g + 1
            n, i = (3 * g + PARTS.index(key[2]), key[3]) if kind == "A" else (3 * NCHUNK + g, key[2])
            if i < 3:
                return w_used, 3 * n + i + 1
            return (proj_done, TB * (n + 1)) if kind == "A" else (z1_done, TB * (g + 1))

        def mask_of(g, b):
            if g == 0:
                return mask0[:, 0 if b == 0 else (2 if b == TB - 1 else 1), :]
            return mask1[:, b % 2, :] if g == 1 else mask2[:, :]

        def key_cols(g, b):
            if g == 0:
                return P * b, 256
            if g == 1:
                return SIDE + 256 * (b // 2), 256
            return SIDE + P * b, P

        def value_blocks(g, b):
            return [(b - 1) % TB, b] if g == 0 else ([b - b % 2, b - b % 2 + 1] if g == 1 else [b])

        def tokens(t, kd, g, b, part):
            if g == 0:
                s = P * b + (SIDE if part == V else 0)
                return t[:, kd, s:s + P]
            s = b // 2 + 4 * P * (b % 2) if g == 1 else b
            return t[:, kd, s:s + STRIDE[g] * (P - 1) + 1:STRIDE[g]]

        def tile_at(t):
            return t // (3 * TB), PARTS[t // TB % 3], t % TB

        FIRST = (0, 1, 3, 4, 5, 6, 7)
        LEAD = 5

        def tile_bank(t):
            return bank(FIRST[t % len(FIRST)] if t < 2 * TB else t % 2)

        def bank_before(t):
            return t - len(FIRST) if t < 2 * TB else t - 2

        def transposed_in(t):
            n = t - LEAD if 0 <= t - LEAD < TB else t - 2
            return n if 0 <= n < NT and tile_at(n)[1] == K and (n >= TB or t == n + LEAD) else None

        def qk_number(c, part, b):
            return 2 * TB * c + (TB if part == Q else 0) + b

        NT = NCHUNK * 3 * TB

        def attended(t):
            t -= 2
            if 0 <= t < NT and tile_at(t)[1] == Q:
                return TB * (t // (3 * TB)) + t % TB
            return None

        def slots(t):
            a, z = attended(t), attended(t - 1)
            for i in range(4):
                s = 4 * a + i if a is not None else None
                if s is not None:
                    first = 4 * TB * (a // TB)
                    yield s, s - 1 if s > first else None, s - 2 if s > first + 1 else None
                elif z is not None and i < 2:
                    yield None, 4 * z + 3 if i == 0 else None, 4 * z + 2 + i
                else:
                    yield None, None, None

        def block_at(n):
            return n // (HALF * TB), n % HALF, n // HALF % TB

        block = ctx.enter_context(nc.Block())

        v_steps = [t + 1 for t in range(NT // 2, NT) if tile_at(t)[1] == V]
        factor_step = v_steps[0]
        merge_at = {v_steps[2 * m + 2]: m for m in range(H)}

        def merge_buffer(m):
            if m < H:
                return uf, uf_in[0], 16 * (NA + 1) * (m + 1)
            i = m - H
            n = i // 2 + (1 if i % 2 else H + 1)
            return (uf, uf2)[i % 2], uf_in[i % 2], 16 * (NA + 1) * n

        @block.sync
        def _(sp):
            def load_stats(half, groups):
                for g in groups:
                    sp.wait_ge(st_out, 16 * 2 * (NA * half + g + 1))
                    for s, t in enumerate((fm, fden)):
                        if g == 0:
                            sp.dma_start(t[:, g, :], st_d[g, s, HALF * half:HALF * half + HALF].rearrange(
                                "h (t j) -> (h t) j", t=TB)).then_inc(f_in, 16)
                            continue
                        for h in range(HALF):
                            src = st_d[g, s, HALF * half + h].rearrange("(r t j) -> t r j", r=STRIDE[g], t=TB)
                            dst = t[TB * h:TB * h + TB, g, :].rearrange("p (r j) -> p r j", r=STRIDE[g])
                            sp.dma_start(dst, src).then_inc(f_in, 16)

            def store_factors(half):
                sp.wait_ge(f_ready, half + 1)
                for g in range(NA):
                    sp.dma_start(f_d[g, HALF * half:HALF * half + HALF].rearrange("h (t q) -> (h t) q", q=P),
                                 fden[:, g, :]).then_inc(f_out, 16)
                sp.wait_ge(f_out, 16 * NA * (half + 1))

            def load_outputs(m):
                h, hf = m // 2, m % 2
                buf, arrived, _ = merge_buffer(m)
                if m == 0:
                    for i in range(2):
                        sp.wait_ge(u_out[i], 16 * NA * TB // 2)
                elif m < H:
                    sp.wait_ge(o_out, 16 * m)
                elif m == H:
                    for i in range(2):
                        sp.wait_ge(u_out[i], 16 * NCHUNK * TB // 2)
                elif m == H + 1:
                    sp.wait_ge(st_out, 16 * 2 * NCHUNK)
                else:
                    sp.wait_ge(merged, m - 1)
                for g in range(NA):
                    r = STRIDE[g]
                    src = u_d[g, h].rearrange("e (r f j) -> e r f j", r=r, f=2)[:, :, hf, :]
                    sp.dma_start(buf[:, g, :].rearrange("p (r j) -> p r j", r=r), src).then_inc(arrived, 16)

            def load_factors(m):
                h, hf = m // 2, m % 2
                buf, arrived, _ = merge_buffer(m)
                sp.dma_start(buf[:, NA:2 * NA, :],
                             f_d[:, h, 512 * hf:512 * hf + 512].unsqueeze(0).to_broadcast([P, NA, 512])).then_inc(arrived, 16)

            def load_merge(m):
                load_outputs(m)
                load_factors(m)

            def store_merged(m):
                h, hf = m // 2, m % 2
                sp.wait_ge(merged, m + 1)
                sp.dma_start(o_d[h, :, 512 * hf:512 * hf + 512], uf[:, 0, :]).then_inc(o_out, 16)

            def exchange(*ms):
                for m in ms:
                    store_merged(m)
                    load_merge(m + 1)

            for u, (src, k, n) in enumerate(units):
                if u >= RAW:
                    sp.wait_ge(w_lo, u - RAW + 1)
                sp.dma_start(raw[:, u % RAW, :].rearrange("p (k c) -> p k c", k=k), src).then_inc(raw_in[u % RAW], 16)
                key = key_of[u]
                if key == ("A", NA, V, 3):
                    load_stats(0, range(NA))
                    store_factors(0)
                    load_merge(0)
                elif key == ("A", NA, Q, 1):
                    exchange(0)
                elif key == ("A", NA, Q, 3):
                    exchange(1, 2)
                elif key == ("A", NA + 1, V, 3):
                    exchange(3)
                elif key == ("A", NA + 1, Q, 1):
                    exchange(4)
                elif key == ("A", NA + 1, Q, 3):
                    exchange(5, 6)
                elif key == ("A", NA + 2, V, 3):
                    store_merged(H - 1)
                    sp.wait_ge(o_out, 16 * H)
                    load_stats(1, (0, 1))
                elif key == ("Y", 5):
                    load_outputs(H)
                    load_stats(1, (2,))
                    load_outputs(H + 1)
                    store_factors(1)
                    load_factors(H)
                    load_factors(H + 1)
                    load_merge(H + 2)
                    load_merge(H + 3)
                elif key == ("Y", 6):
                    load_merge(H + 4)
                    load_merge(H + 5)
                elif key == ("Y", 7):
                    load_merge(H + 6)
                    load_merge(H + 7)

        @block.gpsimd
        def _(pool):
            nc.gpsimd.memset(zero[:, :], 0.0).then_inc(zero_set, 1)
            pool.wait_ge(zero_set, 1)
            for u in range(NU):
                pool.wait_ge(raw_in[u % RAW], 16 * (u // RAW + 1))
                if u < UNITS0:
                    if u >= R0:
                        pool.wait_ge(*unit_released(u - R0))
                elif u < UNITS0 + R1:
                    if u < UNITS0 + 4:
                        pool.wait_ge(m_done, GB * NG)
                    else:
                        pool.wait_ge(*unit_released(UNITS0 - 1))
                else:
                    pool.wait_ge(*unit_released(u - R1))
                w = w0 if u < UNITS0 else w1
                hi, lo = w[:, slot(u), 0, :], w[:, slot(u), 1, :]
                r = raw[:, u % RAW, :]
                nc.gpsimd.tensor_tensor(hi, r, zero[:, 0:1].to_broadcast([P, 1024]), ALU.add).then_inc(w_hi, 1)
                pool.wait_ge(w_hi, u + 1)
                nc.gpsimd.tensor_tensor(lo, r, hi.bitcast(F32), ALU.subtract).then_inc(w_lo, 1)

        @block.tensor
        def _(pe):
            def three(out, lh, ll, rh, rl, first, last):
                nc.tensor.matmul(out, lh, rh, start=first, stop=False)
                nc.tensor.matmul(out, lh, rl, start=False, stop=False)
                return nc.tensor.matmul(out, ll, rh, start=False, stop=last)

            def transpose_x(layer, tb):
                n = layer * TB + tb
                pe.wait_ge(xn_done, n + 1)
                if tb:
                    pe.wait_ge(hlo_done, n)
                elif layer:
                    pe.wait_ge(*released(before["x"]))
                buf = (bufU, bufS)[tb % 2]
                for kd in range(KD):
                    last = nc.tensor.transpose(pair[3][:, kd * P:kd * P + P], buf[:, kd * P:kd * P + P], ident[:, :])
                last.then_inc(xt_done, 1)

            def features_by_tokens(u, pr, kdn, rh, rl, col=0):
                wh, wl = wview(u, False), wview(u, True)
                for kd in range(kdn):
                    for hf in range(2):
                        last = three(pair[pr][:, 512 * hf:512 * hf + 512], wh[:, kd, col:col + P],
                                     wl[:, kd, col:col + P], rh(kd, hf), rl(kd, hf), kd == 0, kd == kdn - 1)
                return last

            def tok(t):
                return lambda kd, hf: t[:, kd, 512 * hf:512 * hf + 512]

            pe.wait_ge(const_in, 16 * 3)
            transpose_x(0, 0)
            transpose_x(0, 1)
            for q in range(4):
                quarter = slice(256 * q, 256 * q + 256)
                for c in range(3):
                    if c == 0:
                        pe.wait_ge(hlo_done, 2 * q + 2)
                    if q == 0:
                        pe.wait_ge(w_lo, c + 1)
                    wh, wl = wview(unit_of[("U", 0, c)], False), wview(unit_of[("U", 0, c)], True)
                    for kd in range(KD):
                        last = three(pair[c][:, quarter], wh[:, kd, :], wl[:, kd, :], hTh[:, kd, quarter],
                                     hTl[:, kd, quarter], kd == 0, kd == KD - 1)
                    if q == 3:
                        last.then_inc(u_done, 1)
                    elif c < 2:
                        transpose_x(0, 2 * q + 2 + c)
            X_AFTER = (3, 4, 6, 7)
            for n, job in enumerate(jobs):
                if n < 3:
                    continue
                if before[job]:
                    pe.wait_ge(*released(before[job]))
                kind, g = job[0], job[1]
                pr = pair_of[job]
                if kind in "UG":
                    u = unit_of[job]
                    pe.wait_ge(w_lo, u + 1)
                    last = features_by_tokens(u, pr, KD, tok(hTh), tok(hTl))
                    last.then_inc(u_done if kind == "U" else g_done, 1)
                elif kind == "M":
                    c = job[2]
                    u = unit_of[("M", g, c // 2)]
                    pe.wait_ge(w_lo, u + 1)
                    pe.wait_ge(diff_done, GB * (g + 1))
                    last = features_by_tokens(u, pr, GB, tok(diffh), tok(diffl), P * (c % 2))
                    last.then_inc(m_done, 1)
                else:
                    po, tb = job[2], job[3]
                    us = [unit_of[("O", g, po, i)] for i in range(2)]
                    if tb == 0:
                        pe.wait_ge(w_lo, us[1] + 1)
                        pe.wait_ge(z_done, GB * g + 2 * po + 2)
                    for i in range(2):
                        for hf in range(2):
                            last = three(pair[pr][:, 512 * hf:512 * hf + 512], zh[:, i, P * tb:P * tb + P],
                                         zl[:, i, P * tb:P * tb + P], wview(us[i], False)[:, 0, 512 * hf:512 * hf + 512],
                                         wview(us[i], True)[:, 0, 512 * hf:512 * hf + 512], i == 0, i == 1)
                    last.then_inc(o_done, 1)
                    if (g, po) == (NG - 1, 1) and tb in X_AFTER:
                        transpose_x(1, X_AFTER.index(tb))

            def project(t, i):
                c, part, b = tile_at(t)
                u = unit_of[("A", c, part, i)]
                if i == 0 and t == TB:
                    pe.wait_ge(hpad_done, 2)
                if i == 0 and bank_before(t) >= 0:
                    cc, pp_, bb = tile_at(bank_before(t))
                    if pp_ == V:
                        pe.wait_ge(v_done, TB * cc + bb + 1)
                    else:
                        pe.wait_ge(qn_done, qk_number(cc, pp_, bb) + 1)
                if b == 0:
                    pe.wait_ge(w_lo, u + 1)
                for k in range(2):
                    kd = 2 * i + k
                    last = three(tile_bank(t), tokens(hTh, kd, c % NA, b, part), tokens(hTl, kd, c % NA, b, part),
                                 wview(u, False)[:, k, :], wview(u, True)[:, k, :], kd == 0, kd == KD - 1)
                if i == 3:
                    last.then_inc(proj_done, 1)
                elif b == TB - 1:
                    last.then_inc(w_used, 1)

            def transpose_qk(t):
                c, part, b = tile_at(t)
                n = qk_number(c, part, b)
                pe.wait_ge(rope_done, n + 1)
                if n:
                    pe.wait_ge(qkT_done, n)
                for h in range(HALF):
                    last = nc.tensor.transpose(bank(2)[:, P * h:P * h + P], qn[:, n % 2, P * h:P * h + P], ident[:, :])
                last.then_inc(qt_done, 1)

            def scores(n):
                c, h, b = block_at(n)
                pe.wait_ge(qkT_done, qk_number(c, Q, b) + 1)
                if n >= 2:
                    pe.wait_ge(masked, n - 1)
                k0, kn = key_cols(c % NA, b)
                nc.tensor.matmul(bank(5 + n % 2)[:, 0:kn], qT[:, b % 2, h, :], kT[:, h, k0:k0 + kn],
                                 start=True, stop=True).then_inc(s_done, 1)

            def transpose_p(n):
                c, h, b = block_at(n)
                pe.wait_ge(p_done, n + 1)
                if n >= 2:
                    pe.wait_ge(pt_ready, n - 1)
                for i in range(key_cols(c % NA, b)[1] // P):
                    last = nc.tensor.transpose(bank(3 + n % 2)[:, P * i:P * i + P], pp[:, n % 2, P * i:P * i + P],
                                               ident[:, :])
                last.then_inc(ptr_done, 1)

            def values(n):
                c, h, b = block_at(n)
                if b == 0 and h == 0:
                    pe.wait_ge(v_done, TB * (c + 1))
                pe.wait_ge(pt_ready, n + 1)
                if h == 0 and n:
                    pe.wait_ge(u_evac, n // HALF)
                vb = value_blocks(c % NA, b)
                for i, v in enumerate(vb):
                    last = nc.tensor.matmul(bank(7)[:, P * h:P * h + P], vv[:, v, HD * h:HD * h + HD],
                                            pt[:, n % 2, P * i:P * i + P], start=(i == 0), stop=(i == len(vb) - 1))
                last.then_inc(pv_done, 1)

            pe.wait_ge(o_added, 2 * TB * NG)
            for t in range(TB // 2):
                pe.wait_ge(hlo_done, TB + t + 1)
                for i in range(4):
                    project(t, i)
                transpose_x(1, TB // 2 + t)
            for t in range(TB // 2, NT + 3):
                for i, (s, tp, pv) in enumerate(slots(t)):
                    if t < NT:
                        if t == TB // 2 and i == 0:
                            pe.wait_ge(hlo_done, 2 * TB)
                        project(t, i)
                    if i == 1 and transposed_in(t) is not None:
                        transpose_qk(transposed_in(t))
                    if s is not None:
                        scores(s)
                    if tp is not None:
                        transpose_p(tp)
                    if pv is not None:
                        values(pv)
                if attended(t) is None and attended(t - 1) is not None:
                    pe.wait_ge(qkT_done, qk_number(*tile_at(min(t - 2, NT - 1))) + 1)
                    nc.tensor.transpose(bank(2)[0:2 * HALF * TB, 0:P],
                                        stat[:, :, :, :].rearrange("p s h b -> p (s h b)"),
                                        ident[:, :]).then_inc(stT_done, 1)
                    pe.wait_ge(st_evac, attended(t - 1) // TB + 1)
                if 1 <= t <= NT and tile_at(t - 1)[1] == Q:
                    transpose_qk(t - 1)

            for h in range(H):
                u = unit_of[("Y", h)]
                pe.wait_ge(w_lo, u + 1)
                if h == 3:
                    pe.wait_ge(u_evac, NCHUNK * TB)
                elif h > 3:
                    pe.wait_ge(ysilu_done, h - 3)
                last = features_by_tokens(u, h % 4, KD, tok(hTh), tok(hTl))
                last.then_inc(yg_done, 1)
            for hf in range(2):
                for tb in range(TB):
                    n = hf * TB + tb
                    if tb == 0:
                        pe.wait_ge(w_lo, unit_of[("Z", hf, 3)] + 1)
                    if n == 0:
                        pe.wait_ge(ysilu_done, H - 3)
                    if n == TB // 2:
                        pe.wait_ge(y_done, 2 * H)
                    if n >= 2:
                        pe.wait_ge(out_ready, n - 1)
                    for i in range(4):
                        u = unit_of[("Z", hf, i)]
                        for k in range(2):
                            hh = 2 * i + k
                            if n == 0:
                                pe.wait_ge(y_done, 2 * hh + 1)
                            last = three(bank(n % 2), yh[:, hh, P * tb:P * tb + P], yl[:, hh, P * tb:P * tb + P],
                                         wview(u, False)[:, k, :], wview(u, True)[:, k, :], hh == 0, hh == H - 1)
                        if tb == TB - 1 and i < 3:
                            last.then_inc(w_used, 1)
                    last.then_inc(z1_done, 1)

        @block.vector
        def _(dve):
            steps = [0]

            def link(ins):
                steps[0] += 1
                ins.then_inc(dve_step, 1)
                dve.wait_ge(dve_step, steps[0])

            def inverse_root(v, t, y):
                link(nc.vector.tensor_scalar(y.bitcast(I32), v.bitcast(I32), -0.5, float(0x5F3759DF),
                                             ALU.mult, ALU.add))
                for _ in range(3):
                    link(nc.vector.scalar_tensor_tensor(out=t, in0=y, scalar=-0.5, in1=y, op0=ALU.mult, op1=ALU.mult))
                    link(nc.vector.tensor_tensor(t, t, v, ALU.mult))
                    link(nc.vector.scalar_tensor_tensor(out=y, in0=t, scalar=1.5, in1=y, op0=ALU.add, op1=ALU.mult))

            def add_out(g, po, tbs=range(TB)):
                for tb in tbs:
                    n = 2 * TB * g + TB * po + tb
                    dve.wait_ge(o_done, n + 1)
                    nc.vector.tensor_tensor(xs[:, tb, :], pair[pair_of[("O", g, po, tb)]][:, :], xs[:, tb, :],
                                            ALU.add).then_inc(o_added, 1)

            def norm_x(layer):
                def lows(tb):
                    n = layer * TB + tb
                    dve.wait_ge(hhi_done, n + 1)
                    nc.vector.tensor_tensor(hTl[:, :, P * tb:P * tb + P],
                                            pair[3][:, :].rearrange("p (k c) -> p k c", k=KD),
                                            hTh[:, :, P * tb:P * tb + P].bitcast(F32), ALU.subtract).then_inc(hlo_done, 1)

                for tb in range(TB):
                    n = layer * TB + tb
                    if layer:
                        add_out(NG - 1, 1, ((0,), (1,), (2, 3), (4, 5), (6, 7), (), (), ())[tb])
                    if tb == 0:
                        dve.wait_ge(nw_in, 16 * (layer + 1))
                    dve.wait_ge(sq_done, n + 1)
                    c = slice(tb, tb + 1)
                    link(nc.vector.tensor_scalar(var[:, c], ss[:, c], 1.0 / D, EPS, ALU.mult, ALU.add))
                    inverse_root(var[:, c], tmp[:, c], rstd[:, c])
                    buf = (bufU, bufS)[tb % 2]
                    nc.vector.scalar_tensor_tensor(out=buf[:, 0:D], in0=xs[:, tb, :], scalar=rstd[:, c],
                                                   in1=bufG[:, :], op0=ALU.mult, op1=ALU.mult).then_inc(xn_done, 1)
                    if tb >= 1:
                        lows(tb - 1)
                lows(TB - 1)
                if layer == 1:
                    dve.wait_ge(hlo_done, TB + 1)
                    nc.vector.tensor_copy(hTl[:, :, T:TPAD], hTl[:, :, 0:SIDE].bitcast(F32)).then_inc(hpad_done, 1)

            norm_x(0)
            dve.wait_ge(const_in, 16 * 3)

            def pool_block(g, c):
                n = GB * g + c
                w = WINDOWS[g]
                dve.wait_ge(u_copied, n + 1)
                src, dst, k = bufU, bufS, 1
                while k < w:
                    ext = w // 2 - k
                    lo, num = PAD - ext, T + 2 * ext
                    s = max(k // 2, 1)
                    a, b = (-1, 0) if k == 1 else (-s, s)
                    link(nc.vector.tensor_tensor(dst[:, lo:lo + num], src[:, lo + a:lo + a + num],
                                                 src[:, lo + b:lo + b + num], ALU.add))
                    src, dst, k = dst, src, 2 * k
                ends = src[:, PAD:PAD + T].rearrange("p (a b) -> p a b", b=8)[:, 0:TB * 16:TB * 16 - 1, :]
                link(nc.vector.tensor_tensor(ends, ends, edge[:, g, :, :], ALU.mult))
                mid = src[:, PAD:PAD + T]
                nc.vector.scalar_tensor_tensor(out=mid, in0=mid, scalar=1.0 / w, in1=pair[pair_of[("U", g, c)]][:, :],
                                               op0=ALU.mult, op1=ALU.subtract).then_inc(d_ready, 1)
                dve.wait_ge(dhi_done, n + 1)
                nc.vector.tensor_tensor(diffl[:, c, :], mid, diffh[:, c, :].bitcast(F32),
                                        ALU.subtract).then_inc(diff_done, 1)
                if w >= 8:
                    link(nc.vector.memset(bufU[:, 0:PAD], 0.0))
                    link(nc.vector.memset(bufU[:, PAD + T:], 0.0))

            def z_block(g, c):
                n = GB * g + c
                dve.wait_ge(silu_done, n + 1)
                dve.wait_ge(m_done, n + 1)
                nc.vector.scalar_tensor_tensor(out=bufG[:, :], in0=pair[pair_of[("M", g, c)]][:, :],
                                               scalar=pscale[:, n:n + 1], in1=bufG[:, :], op0=ALU.mult,
                                               op1=ALU.mult).then_inc(z_ready, 1)
                dve.wait_ge(zhi_done, n + 1)
                nc.vector.tensor_tensor(zl[:, c % 2, :], bufG[:, :], zh[:, c % 2, :].bitcast(F32),
                                        ALU.subtract).then_inc(z_done, 1)

            dve.wait_ge(xt_done, TB)
            link(nc.vector.memset(bufU[:, 0:PAD], 0.0))
            link(nc.vector.memset(bufU[:, PAD + T:], 0.0))
            for g in range(NG):
                pool_block(g, 0)
                if g:
                    add_out(g - 1, 1)
                for c in range(1, GB):
                    pool_block(g, c)
                z_block(g, 0)
                z_block(g, 1)
                add_out(g, 0)
                z_block(g, 2)
                z_block(g, 3)
            norm_x(1)
            dve.wait_ge(x1_out, 16 * TB)
            dve.wait_ge(acon_in, 16 * 9)
            dve.wait_ge(xn_done, 2 * TB)
            nc.vector.memset(kT[:, :, 0:SIDE], 0.0).then_inc(kpad_set, 1)
            nc.vector.memset(kT[:, :, SIDE + T:], 0.0).then_inc(kpad_set, 1)
            nc.vector.memset(wcol[0:ROPE, :], 1.0).then_inc(wcol_set, 1)

            def fold(g, part):
                i = NA * (part == K) + g
                hr = ROPE // 2
                w = wrow[:, i, :].unsqueeze(1)
                nc.vector.tensor_tensor(cosw[:, :, :], cosb[:, g, :, :], w.to_broadcast([P, TB, ROPE]), ALU.mult)
                nc.vector.tensor_tensor(sinw[:, :, 0:hr], sinb[:, g, :, 0:hr],
                                        w[:, :, hr:].to_broadcast([P, TB, hr]), ALU.mult)
                link(nc.vector.tensor_tensor(sinw[:, :, hr:], sinb[:, g, :, hr:],
                                             w[:, :, 0:hr].to_broadcast([P, TB, hr]), ALU.mult))

            def norm_scale(t):
                n = qk_number(*tile_at(t))
                x4 = qn[:, n % 2, :].rearrange("p (h e) -> p h e", h=HALF)
                dve.wait_ge(qsq_done, n + 1)
                link(nc.vector.tensor_reduce(qss[:, :], x4, AX_X, ALU.add))
                link(nc.vector.tensor_scalar(qvar[:, :], qss[:, :], 1.0 / HD, EPS, ALU.mult, ALU.add))
                inverse_root(qvar[:, :], qtmp[:, :], qrstd[:, :])

            def norm_apply(t):
                n = qk_number(*tile_at(t))
                x4 = qn[:, n % 2, :].rearrange("p (h e) -> p h e", h=HALF)
                nc.vector.tensor_tensor(x4, tile_bank(t).rearrange("p (h e) -> p h e", h=HALF),
                                        qrstd[:, :].unsqueeze(2).to_broadcast([P, HALF, HD]),
                                        ALU.mult).then_inc(qn_done, 1)
                dve.wait_ge(qn_done, n + 1)

            def rotate(t):
                n, b = qk_number(*tile_at(t)), t % TB
                x4 = qn[:, n % 2, :].rearrange("p (h e) -> p h e", h=HALF)
                hr = ROPE // 2
                cw, sw = cosw[:, b, :].unsqueeze(1), sinw[:, b, :].unsqueeze(1)
                nc.vector.tensor_tensor(ropeA[:, :, :], x4[:, :, 0:ROPE], cw.to_broadcast([P, HALF, ROPE]), ALU.mult)
                nc.vector.tensor_tensor(ropeB[:, :, 0:hr], x4[:, :, hr:ROPE],
                                        sw[:, :, 0:hr].to_broadcast([P, HALF, hr]), ALU.mult)
                link(nc.vector.tensor_tensor(ropeB[:, :, hr:], x4[:, :, 0:hr],
                                             sw[:, :, hr:].to_broadcast([P, HALF, hr]), ALU.mult))
                nc.vector.tensor_tensor(x4[:, :, 0:ROPE], ropeA[:, :, :], ropeB[:, :, :], ALU.add).then_inc(rope_done, 1)

            def row_max(n):
                c, h, b = block_at(n)
                kn = key_cols(c % NA, b)[1]
                dve.wait_ge(s_done, n + 1)
                if n >= 2:
                    dve.wait_ge(ptr_done, n - 1)
                if b == 0 and h == 0 and c:
                    dve.wait_ge(stT_done, c)
                nc.vector.tensor_tensor_reduce(pp[:, n % 2, 0:kn], bank(5 + n % 2)[:, 0:kn], mask_of(c % NA, b), -SCALE,
                                               3e38, ALU.add, ALU.min, stat[:, 0, h, b:b + 1]).then_inc(masked, 1)

            def take_pt(n):
                c, h, b = block_at(n)
                kn = key_cols(c % NA, b)[1]
                dve.wait_ge(ptr_done, n + 1)
                if n >= 2:
                    dve.wait_ge(pv_done, n - 1)
                nc.vector.tensor_copy(pt[:, n % 2, 0:kn], bank(3 + n % 2)[:, 0:kn]).then_inc(pt_ready, 1)

            def grouped(t, g):
                if g == 0:
                    return t[:, g, :]
                return t[:, g, :].rearrange("p (r j) -> p j r", r=STRIDE[g])

            def natural(t2, g):
                return t2 if g == 0 else t2.rearrange("p (j r) -> p j r", r=STRIDE[g])

            def factors(half):
                dve.wait_ge(f_in, 16 * 2 * (1 + (NA - 1) * HALF) * (half + 1))
                link(nc.vector.tensor_copy(ftot, fm[:, 0, :]))
                for g in (1, 2):
                    link(nc.vector.tensor_tensor(natural(ftot, g), natural(ftot, g), grouped(fm, g), ALU.min))
                for g in range(NA):
                    link(nc.vector.tensor_tensor(grouped(fm, g), natural(ftot, g), grouped(fm, g), ALU.subtract))
                nc.vector.memset(ftot, 0.0).then_inc(f_sub, 1)
                dve.wait_ge(f_exp, half + 1)
                dve.wait_ge(f_sub, half + 1)
                for g in range(NA):
                    link(nc.vector.tensor_tensor(fden[:, g, :], fden[:, g, :], fm[:, g, :], ALU.mult))
                    link(nc.vector.tensor_tensor(natural(ftot, g), natural(ftot, g), grouped(fden, g), ALU.add))
                link(nc.vector.reciprocal(ftot, ftot))
                for g in range(NA):
                    last = nc.vector.tensor_tensor(natural(fden[:, g, :], g), grouped(fm, g), natural(ftot, g),
                                                   ALU.mult)
                last.then_inc(f_ready, 1)

            def merge(m):
                buf, arrived, n = merge_buffer(m)
                dve.wait_ge(arrived, n)
                for g in range(NA):
                    if g == 0:
                        a, f = buf[:, 0, :], buf[:, NA, :]
                    else:
                        a = buf[:, g, :].rearrange("p (r j) -> p j r", r=STRIDE[g])
                        f = buf[:, NA + g, :].rearrange("p (j r) -> p j r", r=STRIDE[g])
                    op = nc.vector.tensor_tensor(f, a, f, ALU.mult)
                link(op)
                h, hf = m // 2, m % 2
                out = uf[:, 0, :] if m < H else mixed[:, h, 512 * hf:512 * hf + 512]
                link(nc.vector.tensor_tensor(buf[:, NA, :], buf[:, NA, :], buf[:, NA + 1, :], ALU.add))
                nc.vector.tensor_tensor(out, buf[:, NA, :], buf[:, NA + 2, :], ALU.add).then_inc(merged, 1)

            for t in range(NT + 3):
                c, part, b = tile_at(t - 1) if 1 <= t <= NT else (0, V, 1)
                stages = []
                if part != V:
                    if b == 0:
                        fold(c % NA, part)
                    stages = [norm_scale, norm_apply, rotate]
                for i, (s, tp, pv) in enumerate(slots(t)):
                    if s is not None:
                        row_max(s)
                    if tp is not None:
                        take_pt(tp)
                    if i < len(stages):
                        stages[i](t - 1)
                if t == factor_step:
                    factors(0)
                if t in merge_at:
                    merge(merge_at[t])

            factors(1)
            dve.wait_ge(pv_done, NCHUNK * TB * HALF)
            dve.wait_ge(st_out, 16 * 2 * NCHUNK)
            for i in range(2):
                dve.wait_ge(u_out[i], 16 * NCHUNK * TB // 2)
            for h in range(H):
                if h < HALF:
                    merge(H + 2 * h)
                    merge(H + 2 * h + 1)
                    dve.wait_ge(o_in[h], 16)
                else:
                    dve.wait_ge(merged, 2 * h + 2)
                dve.wait_ge(ysilu_done, h + 1)
                if h:
                    dve.wait_ge(y_done, 2 * h)
                for hf in range(2):
                    half_ = slice(512 * hf, 512 * hf + 512)
                    nc.vector.tensor_tensor(yo[:, hf, :], mixed[:, h, half_], gate[:, h, half_],
                                            ALU.mult).then_inc(y_ready, 1)
                for hf in range(2):
                    half_ = slice(512 * hf, 512 * hf + 512)
                    dve.wait_ge(yhi_done, 2 * h + hf + 1)
                    nc.vector.tensor_tensor(yl[:, h, half_], yo[:, hf, :], yh[:, h, half_].bitcast(F32),
                                            ALU.subtract).then_inc(y_done, 1)

            for n in range(2 * TB):
                dve.wait_ge(x1_in[n % 3], 16 * (n // 3 + 1))
                dve.wait_ge(z1_done, n + 1)
                s = n % 3
                nc.vector.tensor_tensor(uf[:, s, :], bank(n % 2), uf[:, s, :], ALU.add).then_inc(out_ready, 1)

        @block.scalar
        def _(act):
            steps = [0]
            act.dma_start(xs[:, 0, :], x2[0:P, :]).then_inc(xin[0], 16)
            act.dma_start(bufG[:, :], pool_norm[0:1, :].to_broadcast([P, D])).then_inc(nw_in, 16)
            act.dma_start(ident[:, :], ident_d).then_inc(const_in, 16)
            for tb in range(1, TB):
                act.dma_start(xs[:, tb, :], x2[P * tb:P * tb + P, :]).then_inc(xin[tb], 16)
            act.dma_start(pscale[:, :], pool_scale[0].rearrange("(c p) -> p c", p=P),
                          allow_slow_non_contiguous=True).then_inc(const_in, 16)
            act.dma_start(edge[:, :, :, :].rearrange("p g a b -> p (g a b)"),
                          edge_d.to_broadcast([P, NG * 16])).then_inc(const_in, 16)

            def load_tables():
                act.dma_start(cosb[:, :, :, :], cos_d.rearrange("g (b p) e -> p g b e", p=P)).then_inc(acon_in, 16)
                act.dma_start(sinb[:, :, :, :], sin_d.rearrange("g (b p) e -> p g b e", p=P)).then_inc(acon_in, 16)
                wr = wrow[:, :, :].rearrange("p (k g) e -> p k g e", k=2)
                wc = wcol[ROPE:P, :].rearrange("p (k g) -> p k g", k=2)
                for k, w in enumerate((att_q_norm, att_k_norm)):
                    act.dma_start(wr[:, k], w[0:1, :, 0:ROPE].to_broadcast([P, NA, ROPE])).then_inc(acon_in, 16)
                    act.dma_start(wc[:, k], w[0, :, ROPE:HD].rearrange("g e -> e g"),
                                  allow_slow_non_contiguous=True).then_inc(acon_in, 16)
                act.dma_start(mask0[:, :, :], mask0_d.rearrange("m p c -> p m c")).then_inc(acon_in, 16)
                act.dma_start(mask1[:, :, :], mask1_d.rearrange("m p c -> p m c")).then_inc(acon_in, 16)
                act.dma_start(mask2[:, :], mask2_d).then_inc(acon_in, 16)

            def norm_x(layer):
                def highs(tb):
                    n = layer * TB + tb
                    act.wait_ge(xt_done, n + 1)
                    nc.scalar.activation(hTh[:, :, P * tb:P * tb + P],
                                         pair[3][:, :].rearrange("p (k c) -> p k c", k=KD),
                                         ACT.Copy).then_inc(hhi_done, 1)

                for tb in range(TB):
                    n = layer * TB + tb
                    if layer == 0:
                        act.wait_ge(xin[tb], 16)
                    else:
                        act.wait_ge(o_added, 2 * TB * NG - TB + tb + 1)
                        act.dma_start(x1_d[P * tb:P * tb + P, :], xs[:, tb, :]).then_inc(x1_out, 16)
                        if tb == 5:
                            act.wait_ge(o_added, 2 * TB * NG)
                            load_tables()
                    if tb >= 2:
                        act.wait_ge(xt_done, n - 1)
                    buf = (bufU, bufS)[tb % 2]
                    nc.scalar.activation(buf[:, 0:D], xs[:, tb, :], ACT.Square,
                                         accum_out=ss[:, tb:tb + 1]).then_inc(sq_done, 1)
                    if tb >= 1:
                        highs(tb - 1)
                highs(TB - 1)
                if layer == 1:
                    act.wait_ge(hhi_done, TB + 1)
                    nc.scalar.activation(hTh[:, :, T:TPAD], hTh[:, :, 0:SIDE].bitcast(F32),
                                         ACT.Copy).then_inc(hpad_done, 1)

            norm_x(0)
            for g in range(NG):
                for c in range(GB):
                    n = GB * g + c
                    act.wait_ge(u_done, n + 1)
                    if n == 0:
                        act.wait_ge(xt_done, TB)
                    else:
                        act.wait_ge(diff_done, n)
                    nc.scalar.activation(bufU[:, PAD:PAD + T], pair[pair_of[("U", g, c)]][:, :],
                                         ACT.Copy).then_inc(u_copied, 1)
                    act.wait_ge(d_ready, n + 1)
                    if g:
                        act.wait_ge(m_done, GB * g)
                    fin = bufU if g % 2 else bufS
                    nc.scalar.activation(diffh[:, c, :], fin[:, PAD:PAD + T], ACT.Copy).then_inc(dhi_done, 1)
                for c in range(GB):
                    n = GB * g + c
                    act.wait_ge(g_done, n + 1)
                    if n == 0:
                        act.wait_ge(xn_done, TB)
                    else:
                        act.wait_ge(z_done, n)
                    nc.scalar.activation(bufG[:, :], pair[pair_of[("G", g, c)]][:, :], ACT.Silu).then_inc(silu_done, 1)
                    act.wait_ge(z_ready, n + 1)
                    if n >= 2:
                        act.wait_ge(o_done, 2 * TB * ((n - 2) // GB) + TB * ((n - 2) % GB // 2) + TB)
                    nc.scalar.activation(zh[:, c % 2, :], bufG[:, :], ACT.Copy).then_inc(zhi_done, 1)

            act.wait_ge(z_done, GB * NG)
            act.dma_start(bufG[:, :], att_norm[0:1, :].to_broadcast([P, D])).then_inc(nw_in, 16)
            norm_x(1)
            act.wait_ge(x1_out, 16 * TB)
            act.wait_ge(acon_in, 16 * 9)
            act.wait_ge(wcol_set, 1)
            act.wait_ge(kpad_set, 2)

            def square(t):
                n = qk_number(*tile_at(t))
                act.wait_ge(proj_done, t + 1)
                if n >= 2:
                    act.wait_ge(qt_done, n - 1)
                nc.scalar.activation(qn[:, n % 2, :], tile_bank(t), ACT.Square).then_inc(qsq_done, 1)

            def take_qk(t):
                c, part, b = tile_at(t)
                n = qk_number(c, part, b)
                act.wait_ge(qt_done, n + 1)
                if part == Q:
                    if n >= 2 and TB * c + b >= 2:
                        act.wait_ge(s_done, HALF * (TB * c + b - 1))
                    dst = qT[:, b % 2, :, :]
                else:
                    if b == 0 and c:
                        act.wait_ge(s_done, HALF * TB * c)
                    dst = kT[:, :, SIDE + P * b:SIDE + P * b + P]
                i = NA * (part == K) + c % NA
                nc.scalar.activation(dst, bank(2).rearrange("p (h t) -> p h t", h=HALF), ACT.Copy,
                                     scale=wcol[:, i:i + 1]).then_inc(qkT_done, 1)

            def take_v(t):
                c, part, b = tile_at(t)
                act.wait_ge(proj_done, t + 1)
                if b == 0 and c:
                    act.wait_ge(pv_done, HALF * TB * c)
                nc.scalar.activation(vv[:, b, :], tile_bank(t), ACT.Copy).then_inc(v_done, 1)

            def exps(n):
                c, h, b = block_at(n)
                kn = key_cols(c % NA, b)[1]
                act.wait_ge(masked, n + 1)
                nc.scalar.activation(pp[:, n % 2, 0:kn], pp[:, n % 2, 0:kn], ACT.Exp, bias=stat[:, 0, h, b:b + 1],
                                     scale=-1.0, accum_out=stat[:, 1, h, b:b + 1]).then_inc(p_done, 1)

            def take_u(a):
                c, b = a // TB, a % TB
                act.wait_ge(pv_done, HALF * (a + 1))
                if a >= 2:
                    act.wait_ge(u_out[a % 2], 16 * (a // 2))
                nc.scalar.activation(uo[:, a % 2, :, :], bank(7).rearrange("p (h t) -> p h t", h=HALF),
                                     ACT.Copy).then_inc(u_evac, 1)
                act.wait_ge(u_evac, a + 1)
                h0 = HALF * (c // NA)
                act.dma_start(u_d[c % NA, h0:h0 + HALF, :, P * b:P * b + P].rearrange("h e t -> e h t"),
                              uo[:, a % 2, :, :]).then_inc(u_out[a % 2], 16)

            def take_stat(c):
                act.wait_ge(stT_done, c + 1)
                if c:
                    act.wait_ge(st_out, 16 * 2 * c)
                nc.scalar.activation(statT[:, :], bank(2)[0:2 * HALF * TB, 0:P], ACT.Copy).then_inc(st_evac, 1)
                act.wait_ge(st_evac, c + 1)
                half, g = c // NA, c % NA
                for s in range(2):
                    act.dma_start(st_d[g, s, HALF * half:HALF * half + HALF].rearrange("h (b q) -> (h b) q", q=P),
                                  statT[s * HALF * TB:(s + 1) * HALF * TB, :]).then_inc(st_out, 16)

            def exp_factors(half):
                act.wait_ge(f_sub, half + 1)
                nc.scalar.activation(fm, fm, ACT.Exp).then_inc(f_exp, 1)

            for t in range(NT + 3):
                if 2 <= t <= NT + 1 and tile_at(t - 2)[1] == Q:
                    take_qk(t - 2)
                part = tile_at(t - 1)[1] if 1 <= t <= NT else None
                if part == V:
                    take_v(t - 1)
                elif part is not None:
                    square(t - 1)
                if 2 <= t <= NT + 1 and tile_at(t - 2)[1] == K:
                    take_qk(t - 2)
                z = attended(t - 1)
                for i, (s, tp, pv) in enumerate(slots(t)):
                    if i == 2 and z is not None:
                        take_u(z)
                    if s is not None:
                        exps(s)
                if attended(t) is None and z is not None:
                    take_stat(z // TB)
                if t == factor_step:
                    exp_factors(0)

            act.wait_ge(u_out[0], 16 * NCHUNK * TB // 2)
            act.wait_ge(u_out[1], 16 * NCHUNK * TB // 2)
            act.wait_ge(st_out, 16 * 2 * NCHUNK)
            act.wait_ge(o_out, 16 * H)
            for h in range(HALF):
                act.dma_start(mixed[:, h, :], o_d[h]).then_inc(o_in[h], 16)
            exp_factors(1)

            def load_x1(n):
                if n >= 3:
                    act.wait_ge(out_sent[n % 3], 16 * (n // 3))
                act.dma_start(uf[:, n % 3, :], tile(x1_d, n)).then_inc(x1_in[n % 3], 16)

            def tile(t, n):
                hf, tb = n // TB, n % TB
                return t[P * tb:P * tb + P, 512 * hf:512 * hf + 512]

            for h in range(H):
                act.wait_ge(yg_done, h + 1)
                if h == H - 3:
                    act.wait_ge(merged, 2 * H)
                    for n in range(2):
                        load_x1(n)
                nc.scalar.activation(gate[:, h, :], pair[h % 4][:, :], ACT.Silu).then_inc(ysilu_done, 1)
                for hf in range(2):
                    act.wait_ge(y_ready, 2 * h + hf + 1)
                    nc.scalar.activation(yh[:, h, 512 * hf:512 * hf + 512], yo[:, hf, :], ACT.Copy).then_inc(yhi_done, 1)

            for n in range(2 * TB + 1):
                if 2 <= n < 2 * TB:
                    load_x1(n)
                if n >= 1:
                    act.wait_ge(out_ready, n)
                    act.dma_start(tile(out2, n - 1), uf[:, (n - 1) % 3, :]).then_inc(out_sent[(n - 1) % 3], 16)
            for i in range(3):
                act.wait_ge(out_sent[i], 16 * len(range(i, 2 * TB, 3)))


_INS = ["x", "pool_norm", "pool_w_in", "pool_w_group", "pool_scale", "pool_w_out", "att_norm", "att_w_in",
        "att_q_norm", "att_k_norm", "att_w_out"]


def shape_constants(T):
    import numpy as np
    neg = np.float32(-1e30)
    ident = np.eye(P, dtype=np.float32)
    q, c = np.arange(P)[:, None], np.arange(256)[None, :]
    band = (c - q >= 0) & (c - q <= 2 * SIDE)
    ok0 = np.stack([band & (c >= SIDE), band, band & (c < 256 - SIDE)])
    ok1 = np.stack([np.abs(c - (P * b + q)) <= SIDE for b in range(2)])
    ok2 = (q % 2) == (c[:, :P] % 2)
    masks = [np.where(m, np.float32(0), neg).astype(np.float32) for m in (ok0, ok1, ok2)]
    half = ROPE // 2
    f32 = np.float32
    inv = (f32(1.0) / (f32(500000.0) ** (np.arange(half, dtype=f32) * f32(2.0) / f32(ROPE)))).astype(f32)
    ang = np.arange(T, dtype=f32)[:, None] * inv[None, :]
    cos, sin = np.cos(ang).astype(f32), np.sin(ang).astype(f32)
    edge = np.ones((len(WINDOWS), 2, 8), f32)
    for g, w in enumerate(WINDOWS):
        for i, t in enumerate(list(range(8)) + list(range(T - 8, T))):
            n = min(t - w // 2 + w, T) - max(t - w // 2, 0)
            edge[g, i // 8, i % 8] = f32(w / n)
    order = [np.arange(T).reshape(T // r, r).T.ravel() for r in STRIDE]
    cos, sin = (np.stack([a[o] for o in order]) for a in (cos, sin))
    return {"ident": ident, "mask0": masks[0], "mask1": masks[1], "mask2": masks[2],
            "cos": np.concatenate([cos, cos], 2), "sin": np.concatenate([-sin, sin], 2),
            "edge": edge.reshape(1, -1)}


def kernel(**inputs):
    import numpy as np
    import concourse.bacc as bacc
    from concourse.bass_utils import run_bass_kernel_spmd as run

    nc = bacc.Bacc("TRN2", target_bir_lowering=False, num_devices=1)
    arrays, args = {}, []
    given = {n: np.ascontiguousarray(inputs[n]) for n in _INS}
    given.update(shape_constants(inputs["x"].shape[1]))
    for name, a in given.items():
        arrays[f"in_{name}_dram"] = a
        args.append(nc.dram_tensor(f"in_{name}_dram", a.shape, mybir.dt.from_np(a.dtype), kind="ExternalInput").ap())
    shape = inputs["x"].shape
    args.append(nc.dram_tensor("out_dram", shape, F32, kind="ExternalOutput").ap())
    encoder_program(nc, *args)
    r = run(nc, [arrays], core_ids=[0])
    return r.results[0]["out_dram"]
```

```python
from contextlib import ExitStack

import concourse.bass as bass
from concourse import mybir

F32 = mybir.dt.float32
F32R = mybir.dt.float32r
I32 = mybir.dt.int32
ALU = mybir.AluOpType
ACT = mybir.ActivationFunctionType
AX_X = mybir.AxisListType.X

P = 128
EPS = 1e-6
ROPE = 32
SIDE = 64
STRIDE = (1, 4, 8)
WINDOWS = (2, 4, 8, 16)
PAD = 8


def encoder_program(nc, x, pool_norm, pool_w_in, pool_w_group, pool_scale, pool_w_out, att_norm, att_w_in,
                    att_q_norm, att_k_norm, att_w_out, ident_d, mask0_d, mask1_d, mask2_d, cos_d, sin_d,
                    edge_d, out):
    T, D = x.shape[1], x.shape[2]
    TB, KD = T // P, D // P
    PW = pool_w_out.shape[1]
    NG = len(WINDOWS)
    GB = PW // NG // P
    HD = P
    H = D // HD
    NA = len(STRIDE)
    HALF = 4
    SCALE = float(HD) ** -0.5
    TPAD = T + SIDE
    KW = T + 2 * SIDE
    NCHUNK = (H // HALF) * NA
    Q, K, V = range(3)
    PARTS = (K, V, Q)

    x2 = x[0]
    out2 = out[0]
    w_in0, w_out0 = pool_w_in[0], pool_w_out[0]
    w_in1, w_out1 = att_w_in[0], att_w_out[0]

    x1_d = nc.dram_tensor("x1_spill", (T, D), F32, kind="Internal").ap()
    u_d = nc.dram_tensor("u_spill", (NA, H, P, T), F32, kind="Internal").ap()
    st_d = nc.dram_tensor("stat_spill", (NA, 2, H, T), F32, kind="Internal").ap()
    o_d = nc.dram_tensor("merged_spill", (H, P, T), F32, kind="Internal").ap()
    f_d = nc.dram_tensor("factor_spill", (NA, H, T), F32, kind="Internal").ap()

    def cols(w, j, n, k0, k):
        return w[k0 * P:(k0 + k) * P, j:j + n].rearrange("(k p) c -> p k c", p=P)

    units = []
    unit_of = {}

    def add(key, src, k, n):
        unit_of[key] = len(units)
        units.append((src, k, n))

    for g in range(NG):
        def wout_units(gg, pair):
            for i in range(2):
                add(("O", gg, pair, i), cols(w_out0, 0, D, gg * GB + 2 * pair + i, 1), 1, D)

        def wgroup_unit(pair):
            add(("M", g, pair), cols(pool_w_group[0, g], 256 * pair, 256, 0, GB), GB, 256)

        def win_unit(kind, c):
            add((kind, g, c), cols(w_in0, (g * GB + c) * P + (PW if kind == "G" else 0), P, 0, KD), KD, P)

        win_unit("U", 0)
        if g:
            wout_units(g - 1, 1)
        for c in range(1, GB):
            win_unit("U", c)
        win_unit("G", 0)
        wgroup_unit(0)
        win_unit("G", 1)
        win_unit("G", 2)
        wout_units(g, 0)
        wgroup_unit(1)
        win_unit("G", 3)
    wout_units(NG - 1, 1)
    UNITS0 = len(units)
    for half in range(H // HALF):
        for g in range(NA):
            for part in PARTS:
                base = (g * 3 + part) * D + half * HALF * HD
                for i in range(4):
                    add(("A", half * NA + g, part, i), cols(w_in1, base, HALF * HD, 2 * i, 2), 2, HALF * HD)
    for h in range(H):
        add(("Y", h), cols(w_in1, 3 * NA * D + h * HD, P, 0, KD), KD, P)
    for hf in range(2):
        for i in range(4):
            add(("Z", hf, i), cols(w_out1, hf * 512, 512, 2 * i, 2), 2, 512)
    NU = len(units)
    R0, R1, RAW = 4, 6, 2

    def slot(u):
        return u % R0 if u < UNITS0 else (u - UNITS0) % R1

    ctx = ExitStack()
    with ctx:
        def sb(name, shape, dt, stack=ctx):
            return stack.enter_context(nc.sbuf_tensor(name, shape, dt))

        sems = {}

        def sem(name):
            if name not in sems:
                sems[name] = ctx.enter_context(nc.semaphore(name))
            return sems[name]

        hTh = sb("hTh", [P, KD, TPAD], F32R)
        hTl = sb("hTl", [P, KD, TPAD], F32R)
        raw = sb("raw", [P, RAW, 1024], F32)
        ident = sb("ident", [P, P], F32)
        zero = sb("zero", [P, 1], F32)
        edge = sb("edge", [P, NG, 2, 8], F32)
        pscale = sb("pscale", [P, PW // P], F32)
        ss = sb("ss", [P, TB], F32)
        var = sb("var", [P, TB], F32)
        tmp = sb("tmp", [P, TB], F32)
        rstd = sb("rstd", [P, TB], F32)
        with ExitStack() as l0:
            diff = sb("diff", [P, 2, GB, T], F32R, l0)
            diffh, diffl = diff[:, 0], diff[:, 1]
            w0 = sb("w0", [P, R0, 2, 1024], F32R, l0)
            zh = sb("zh", [P, 2, T], F32R, l0)
            zl = sb("zl", [P, 2, T], F32R, l0)
            xs = sb("xs", [P, TB, D], F32, l0)
            bufU = sb("bufU", [P, T + 2 * PAD], F32, l0)
            bufS = sb("bufS", [P, T + 2 * PAD], F32, l0)
            bufG = sb("bufG", [P, T], F32, l0)
            squares = sb("squares", [P, D], F32, l0)
        with ExitStack() as l1:
            w1 = sb("w1", [P, R1, 2, 1024], F32R, l1)
            uf = sb("uf", [P, 6, 512], F32, l1)
            with ExitStack() as la:
                qn = sb("qn", [P, 2, HALF * HD], F32, la)
                mask0 = sb("mask0", [P, 3, 256], F32, la)
                mask1 = sb("mask1", [P, 2, 256], F32, la)
                mask2 = sb("mask2", [P, P], F32, la)
                cosb = sb("cosb", [P, NA, TB, ROPE], F32, la)
                sinb = sb("sinb", [P, NA, TB, ROPE], F32, la)
                cosw = sb("cosw", [P, TB, ROPE], F32, la)
                sinw = sb("sinw", [P, TB, ROPE], F32, la)
                wrow = sb("wrow", [P, 2 * NA, ROPE], F32, la)
                wcol = sb("wcol", [P, 2 * NA], F32, la)
                ropeA = sb("ropeA", [P, HALF, ROPE], F32, la)
                ropeB = sb("ropeB", [P, HALF, ROPE], F32, la)
                qss = sb("qss", [P, HALF], F32, la)
                qvar = sb("qvar", [P, HALF], F32, la)
                qtmp = sb("qtmp", [P, HALF], F32, la)
                qrstd = sb("qrstd", [P, HALF], F32, la)
                qT = sb("qT", [P, 2, HALF, P], F32, la)
                kT = sb("kT", [P, HALF, KW], F32, la)
                vv = sb("vv", [P, TB, HALF * HD], F32, la)
                uo = sb("uo", [P, 2, HALF, P], F32, la)
                pp = sb("pp", [P, 2, 256], F32, la)
                pt = sb("pt", [P, 2, 256], F32, la)
                stat = sb("stat", [P, 2, HALF, TB], F32, la)
                statT = sb("statT", [2 * HALF * TB, P], F32, la)
            with ExitStack() as ly:
                yh = sb("yh", [P, H, T], F32R, ly)
                yl = sb("yl", [P, H, T], F32R, ly)
                yo = sb("yo", [P, 2, 512], F32, ly)
            with ExitStack() as ly:
                gate = sb("gate", [P, H, T], F32, ly)
                mixed = sb("mixed", [P, H, T], F32, ly)
            fm = uf[0:HALF * TB, NA, 0:NA * P].rearrange("p (g c) -> p g c", g=NA)
            fden = uf[0:HALF * TB, NA + 1, 0:NA * P].rearrange("p (g c) -> p g c", g=NA)
            ftot = uf[0:HALF * TB, NA + 2, 0:P]
            uf2 = gate[:, H - 3:H, :].rearrange("p a (b c) -> p (a b) c", b=2)

        pair = [ctx.enter_context(nc.psum_tensor(f"pair{i}", [P, 1024], F32)) for i in range(4)]

        def bank(i):
            return pair[i // 2][:, 512 * (i % 2):512 * (i % 2) + 512]

        def wview(u, lo):
            src, k, n = units[u]
            t = w0 if u < UNITS0 else w1
            return t[:, slot(u), 1 if lo else 0, :].rearrange("p (k c) -> p k c", k=k)

        xin = [sem(f"xin{i}") for i in range(TB)]
        raw_in = [sem(f"raw_in{i}") for i in range(RAW)]
        w_hi, w_hi_act, w_lo, w_used = sem("w_hi"), sem("w_hi_act"), sem("w_lo"), sem("w_used")
        const_in, ident_in, zero_set = sem("const_in"), sem("ident_in"), sem("zero_set")
        nw_in = sem("nw_in")
        sq_done, xn_done = sem("sq_done"), sem("xn_done")
        xt_done, hhi_done, hlo_done, hpad_done = sem("xt_done"), sem("hhi_done"), sem("hlo_done"), sem("hpad_done")
        u_done, g_done, m_done, o_done = sem("u_done"), sem("g_done"), sem("m_done"), sem("o_done")
        u_copied, d_ready, dhi_done, diff_done = sem("u_copied"), sem("d_ready"), sem("dhi_done"), sem("diff_done")
        silu_done, z_ready, zhi_done, z_done, o_added = (sem("silu_done"), sem("z_ready"), sem("zhi_done"),
                                                         sem("z_done"), sem("o_added"))
        x1_out = sem("x1_out")
        acon_in, kpad_set, wcol_set = sem("acon_in"), sem("kpad_set"), sem("wcol_set")
        proj_done, qsq_done = sem("proj_done"), sem("qsq_done")
        qn_done, rope_done, qt_done, qkT_done, v_done = (sem("qn_done"), sem("rope_done"), sem("qt_done"),
                                                         sem("qkT_done"), sem("v_done"))
        s_done, masked, p_done, ptr_done, pt_ready, pv_done, u_evac = (
            sem("s_done"), sem("masked"), sem("p_done"), sem("ptr_done"), sem("pt_ready"), sem("pv_done"),
            sem("u_evac"))
        u_out = [sem("u_out0"), sem("u_out1")]
        stT_done, st_evac, st_out = sem("stT_done"), sem("st_evac"), sem("st_out")
        f_in, f_sub, f_exp, f_ready, f_out = sem("f_in"), sem("f_sub"), sem("f_exp"), sem("f_ready"), sem("f_out")
        uf_in, merged, o_out = [sem("uf_in0"), sem("uf_in1")], sem("merged"), sem("o_out")
        o_in = [sem(f"o_in{i}") for i in range(HALF)]
        yg_done, ysilu_done, y_ready, yhi_done, y_done = (sem("yg_done"), sem("ysilu_done"), sem("y_ready"),
                                                          sem("yhi_done"), sem("y_done"))
        z1_done, out_ready = sem("z1_done"), sem("out_ready")
        x1_in = [sem(f"x1_in{i}") for i in range(3)]
        out_sent = [sem(f"out_sent{i}") for i in range(3)]
        dve_step, table_loaded = sem("dve_step"), sem("table_loaded")

        jobs = []
        for g in range(NG):
            jobs.append(("U", g, 0))
            if g:
                jobs += [("O", g - 1, 1, tb) for tb in range(TB)]
            jobs += [("U", g, c) for c in range(1, GB)]
            jobs += [("G", g, 0), ("M", g, 0), ("G", g, 1), ("M", g, 1), ("G", g, 2)]
            jobs += [("O", g, 0, tb) for tb in range(TB)]
            jobs += [("M", g, 2), ("G", g, 3), ("M", g, 3)]
        jobs += [("O", NG - 1, 1, tb) for tb in range(TB)]
        pair_of = {j: n % 4 for n, j in enumerate(jobs)}
        for n, j in enumerate(jobs[-TB:]):
            pair_of[j] = n % 3
        users = [None] * 4
        before = {}
        for j in jobs:
            before[j] = users[pair_of[j]]
            users[pair_of[j]] = j
        before["x"] = users[3]

        def released(job):
            kind, g = job[0], job[1]
            if kind == "U":
                return d_ready, GB * g + job[2] + 1
            if kind == "G":
                return silu_done, GB * g + job[2] + 1
            if kind == "M":
                return z_ready, GB * g + job[2] + 1
            return o_added, 2 * TB * g + TB * job[2] + job[3] + 1

        key_of = {n: key for key, n in unit_of.items()}

        def unit_released(u):
            key = key_of[u]
            kind, g = key[0], key[1]
            if kind == "U":
                return u_done, GB * g + key[2] + 1
            if kind == "G":
                return g_done, GB * g + key[2] + 1
            if kind == "M":
                return m_done, GB * g + 2 * key[2] + 2
            if kind == "O":
                return o_done, 2 * TB * g + TB * key[2] + TB
            if kind == "Y":
                return yg_done, g + 1
            n, i = (3 * g + PARTS.index(key[2]), key[3]) if kind == "A" else (3 * NCHUNK + g, key[2])
            if i < 3:
                return w_used, 3 * n + i + 1
            return (proj_done, TB * (n + 1)) if kind == "A" else (z1_done, TB * (g + 1))

        def mask_of(g, b):
            if g == 0:
                return mask0[:, 0 if b == 0 else (2 if b == TB - 1 else 1), :]
            return mask1[:, b % 2, :] if g == 1 else mask2[:, :]

        def key_cols(g, b):
            if g == 0:
                return P * b, 256
            if g == 1:
                return SIDE + 256 * (b // 2), 256
            return SIDE + P * b, P

        def value_blocks(g, b):
            return [(b - 1) % TB, b] if g == 0 else ([b - b % 2, b - b % 2 + 1] if g == 1 else [b])

        def tokens(t, kd, g, b, part):
            if g == 0:
                s = P * b + (SIDE if part == V else 0)
                return t[:, kd, s:s + P]
            s = b // 2 + 4 * P * (b % 2) if g == 1 else b
            return t[:, kd, s:s + STRIDE[g] * (P - 1) + 1:STRIDE[g]]

        def tile_at(t):
            return t // (3 * TB), PARTS[t // TB % 3], t % TB

        FIRST = (0, 1, 3, 4, 5, 6, 7)
        LEAD = 5

        def tile_bank(t):
            return bank(FIRST[t % len(FIRST)] if t < 2 * TB else t % 2)

        def bank_before(t):
            return t - len(FIRST) if t < 2 * TB else t - 2

        def transposed_in(t):
            n = t - LEAD if 0 <= t - LEAD < TB else t - 2
            return n if 0 <= n < NT and tile_at(n)[1] == K and (n >= TB or t == n + LEAD) else None

        def qk_number(c, part, b):
            return 2 * TB * c + (TB if part == Q else 0) + b

        NT = NCHUNK * 3 * TB

        def attended(t):
            t -= 2
            if 0 <= t < NT and tile_at(t)[1] == Q:
                return TB * (t // (3 * TB)) + t % TB
            return None

        def slots(t):
            a, z = attended(t), attended(t - 1)
            for i in range(4):
                s = 4 * a + i if a is not None else None
                if s is not None:
                    first = 4 * TB * (a // TB)
                    yield s, s - 1 if s > first else None, s - 2 if s > first + 1 else None
                elif z is not None and i < 2:
                    yield None, 4 * z + 3 if i == 0 else None, 4 * z + 2 + i
                else:
                    yield None, None, None

        def block_at(n):
            return n // (HALF * TB), n % HALF, n // HALF % TB

        act_units = [unit_of[("A", c, part, 3)] for c in range(NCHUNK) for part in PARTS if c or part == Q]

        block = ctx.enter_context(nc.Block())

        v_steps = [t + 1 for t in range(NT // 2, NT) if tile_at(t)[1] == V]
        factor_step = v_steps[0]
        merge_at = {v_steps[i]: m for m, i in enumerate((2, 5, TB, TB + 3, TB + 6, 2 * TB, 2 * TB + 3, 2 * TB + 6))}

        def merge_buffer(m):
            if m < H:
                return uf, uf_in[0], 16 * (NA + 1) * (m + 1)
            i = m - H
            n = i // 2 + (1 if i % 2 else H + 1)
            return (uf, uf2)[i % 2], uf_in[i % 2], 16 * (NA + 1) * n

        @block.sync
        def _(sp):
            def load_stats(half, groups):
                for g in groups:
                    sp.wait_ge(st_out, 16 * 2 * (NA * half + g + 1))
                    for s, t in enumerate((fm, fden)):
                        if g == 0:
                            sp.dma_start(t[:, g, :], st_d[g, s, HALF * half:HALF * half + HALF].rearrange(
                                "h (t j) -> (h t) j", t=TB)).then_inc(f_in, 16)
                            continue
                        for h in range(HALF):
                            src = st_d[g, s, HALF * half + h].rearrange("(r t j) -> t r j", r=STRIDE[g], t=TB)
                            dst = t[TB * h:TB * h + TB, g, :].rearrange("p (r j) -> p r j", r=STRIDE[g])
                            sp.dma_start(dst, src).then_inc(f_in, 16)

            def store_factors(half):
                sp.wait_ge(f_ready, half + 1)
                for g in range(NA):
                    sp.dma_start(f_d[g, HALF * half:HALF * half + HALF].rearrange("h (t q) -> (h t) q", q=P),
                                 fden[:, g, :]).then_inc(f_out, 16)
                sp.wait_ge(f_out, 16 * NA * (half + 1))

            def load_outputs(m):
                h, hf = m // 2, m % 2
                buf, arrived, _ = merge_buffer(m)
                if m == 0:
                    for i in range(2):
                        sp.wait_ge(u_out[i], 16 * NA * TB // 2)
                elif m < H:
                    sp.wait_ge(o_out, 16 * m)
                elif m == H:
                    for i in range(2):
                        sp.wait_ge(u_out[i], 16 * NCHUNK * TB // 2)
                elif m == H + 1:
                    sp.wait_ge(st_out, 16 * 2 * NCHUNK)
                else:
                    sp.wait_ge(merged, m - 1)
                for g in range(NA):
                    r = STRIDE[g]
                    src = u_d[g, h].rearrange("e (r f j) -> e r f j", r=r, f=2)[:, :, hf, :]
                    sp.dma_start(buf[:, g, :].rearrange("p (r j) -> p r j", r=r), src).then_inc(arrived, 16)

            def load_factors(m):
                h, hf = m // 2, m % 2
                buf, arrived, _ = merge_buffer(m)
                sp.dma_start(buf[:, NA:2 * NA, :],
                             f_d[:, h, 512 * hf:512 * hf + 512].unsqueeze(0).to_broadcast([P, NA, 512])).then_inc(arrived, 16)

            def load_merge(m):
                load_outputs(m)
                load_factors(m)

            def store_merged(m):
                h, hf = m // 2, m % 2
                sp.wait_ge(merged, m + 1)
                sp.dma_start(o_d[h, :, 512 * hf:512 * hf + 512], uf[:, 0, :]).then_inc(o_out, 16)

            def exchange(m):
                store_merged(m)
                load_merge(m + 1)

            for u, (src, k, n) in enumerate(units):
                if u == 0:
                    sp.wait_ge(xin[0], 16)
                if u >= RAW:
                    sp.wait_ge(w_lo, u - RAW + 1)
                sp.dma_start(raw[:, u % RAW, :].rearrange("p (k c) -> p k c", k=k), src).then_inc(raw_in[u % RAW], 16)
                key = key_of[u]
                if key == ("A", NA, V, 3):
                    load_stats(0, range(NA))
                    store_factors(0)
                    load_merge(0)
                elif key == ("A", NA, Q, 1):
                    exchange(0)
                elif key == ("A", NA, Q, 3):
                    exchange(1)
                elif key == ("A", NA + 1, V, 3):
                    exchange(2)
                elif key == ("A", NA + 1, Q, 1):
                    exchange(3)
                elif key == ("A", NA + 1, Q, 3):
                    exchange(4)
                elif key == ("A", NA + 2, V, 3):
                    exchange(5)
                elif key == ("A", NA + 2, Q, 1):
                    exchange(6)
                elif key == ("A", NA + 2, Q, 3):
                    store_merged(H - 1)
                    sp.wait_ge(o_out, 16 * H)
                    load_stats(1, (0, 1))
                elif key == ("Y", 5):
                    load_stats(1, (2,))
                    load_outputs(H)
                    load_outputs(H + 1)
                    store_factors(1)
                    load_factors(H)
                    load_factors(H + 1)
                    load_merge(H + 2)
                    load_merge(H + 3)
                elif key == ("Y", 6):
                    load_merge(H + 4)
                    load_merge(H + 5)
                elif key == ("Y", 7):
                    load_merge(H + 6)
                    load_merge(H + 7)

        @block.gpsimd
        def _(pool):
            nc.gpsimd.memset(zero[:, :], 0.0).then_inc(zero_set, 1)
            pool.wait_ge(zero_set, 1)
            for u in range(NU):
                pool.wait_ge(raw_in[u % RAW], 16 * (u // RAW + 1))
                if u < UNITS0:
                    if u >= R0:
                        pool.wait_ge(*unit_released(u - R0))
                elif u < UNITS0 + R1:
                    if u < UNITS0 + 4:
                        pool.wait_ge(m_done, GB * NG)
                    else:
                        pool.wait_ge(*unit_released(UNITS0 - 1))
                else:
                    pool.wait_ge(*unit_released(u - R1))
                w = w0 if u < UNITS0 else w1
                hi, lo = w[:, slot(u), 0, :], w[:, slot(u), 1, :]
                r = raw[:, u % RAW, :]
                if u in act_units:
                    pool.wait_ge(w_hi_act, act_units.index(u) + 1)
                else:
                    nc.gpsimd.tensor_tensor(hi, r, zero[:, 0:1].to_broadcast([P, 1024]), ALU.add).then_inc(w_hi, 1)
                    pool.wait_ge(w_hi, u + 1 - sum(a < u for a in act_units))
                nc.gpsimd.tensor_tensor(lo, r, hi.bitcast(F32), ALU.subtract).then_inc(w_lo, 1)

        @block.tensor
        def _(pe):
            def three(out, lh, ll, rh, rl, first, last):
                nc.tensor.matmul(out, lh, rh, start=first, stop=False)
                nc.tensor.matmul(out, lh, rl, start=False, stop=False)
                return nc.tensor.matmul(out, ll, rh, start=False, stop=last)

            def transpose_x(layer, tb):
                n = layer * TB + tb
                pe.wait_ge(xn_done, n + 1)
                if tb:
                    pe.wait_ge(hlo_done, n)
                elif layer:
                    pe.wait_ge(*released(before["x"]))
                buf = (bufU, bufS)[tb % 2]
                for kd in range(KD):
                    last = nc.tensor.transpose(pair[3][:, kd * P:kd * P + P], buf[:, kd * P:kd * P + P], ident[:, :])
                last.then_inc(xt_done, 1)

            def features_by_tokens(u, pr, kdn, rh, rl, col=0):
                wh, wl = wview(u, False), wview(u, True)
                for kd in range(kdn):
                    for hf in range(2):
                        last = three(pair[pr][:, 512 * hf:512 * hf + 512], wh[:, kd, col:col + P],
                                     wl[:, kd, col:col + P], rh(kd, hf), rl(kd, hf), kd == 0, kd == kdn - 1)
                return last

            def tok(t):
                return lambda kd, hf: t[:, kd, 512 * hf:512 * hf + 512]

            pe.wait_ge(ident_in, 16)
            transpose_x(0, 0)
            transpose_x(0, 1)
            for q in range(4):
                quarter = slice(256 * q, 256 * q + 256)
                for c in range(3):
                    if c == 0:
                        pe.wait_ge(hlo_done, 2 * q + 2)
                    if q == 0:
                        pe.wait_ge(w_lo, c + 1)
                    wh, wl = wview(unit_of[("U", 0, c)], False), wview(unit_of[("U", 0, c)], True)
                    for kd in range(KD):
                        last = three(pair[c][:, quarter], wh[:, kd, :], wl[:, kd, :], hTh[:, kd, quarter],
                                     hTl[:, kd, quarter], kd == 0, kd == KD - 1)
                    if q == 3:
                        last.then_inc(u_done, 1)
                    elif c < 2:
                        transpose_x(0, 2 * q + 2 + c)
            def output_part(g, po, tb, i):
                u, pr = unit_of[("O", g, po, i)], pair_of[("O", g, po, tb)]
                for hf in range(2):
                    features = slice(512 * hf, 512 * hf + 512)
                    last = three(pair[pr][:, features], zh[:, i, P * tb:P * tb + P], zl[:, i, P * tb:P * tb + P],
                                 wview(u, False)[:, 0, features], wview(u, True)[:, 0, features], i == 0, i == 1)
                return last

            X_AFTER = (3, 4, 5, 7)
            for n, job in enumerate(jobs):
                if n < 3:
                    continue
                if before[job]:
                    pe.wait_ge(*released(before[job]))
                kind, g = job[0], job[1]
                pr = pair_of[job]
                if kind in "UG":
                    u = unit_of[job]
                    pe.wait_ge(w_lo, u + 1)
                    last = features_by_tokens(u, pr, KD, tok(hTh), tok(hTl))
                    last.then_inc(u_done if kind == "U" else g_done, 1)
                elif kind == "M":
                    c = job[2]
                    u = unit_of[("M", g, c // 2)]
                    pe.wait_ge(w_lo, u + 1)
                    pe.wait_ge(diff_done, GB * (g + 1))
                    last = features_by_tokens(u, pr, GB, tok(diffh), tok(diffl), P * (c % 2))
                    last.then_inc(m_done, 1)
                else:
                    po, tb = job[2], job[3]
                    lead = 3 if (g, po) == (NG - 1, 1) else 1
                    if tb == 0:
                        pe.wait_ge(w_lo, unit_of[("O", g, po, 0)] + 1)
                        pe.wait_ge(z_done, GB * g + 2 * po + 1)
                        for ahead in range(lead):
                            if ahead:
                                pe.wait_ge(*released(before[("O", g, po, ahead)]))
                            output_part(g, po, ahead, 0)
                        pe.wait_ge(w_lo, unit_of[("O", g, po, 1)] + 1)
                        pe.wait_ge(z_done, GB * g + 2 * po + 2)
                    if tb >= lead:
                        output_part(g, po, tb, 0)
                    output_part(g, po, tb, 1).then_inc(o_done, 1)
                    if (g, po) == (NG - 1, 1) and tb in X_AFTER:
                        transpose_x(1, X_AFTER.index(tb))

            def project(t, i):
                c, part, b = tile_at(t)
                u = unit_of[("A", c, part, i)]
                if i == 0 and t == TB:
                    pe.wait_ge(hpad_done, 2)
                if i == 0 and bank_before(t) >= 0:
                    cc, pp_, bb = tile_at(bank_before(t))
                    if pp_ == V:
                        pe.wait_ge(v_done, TB * cc + bb + 1)
                    else:
                        pe.wait_ge(qn_done, qk_number(cc, pp_, bb) + 1)
                if b == 0:
                    pe.wait_ge(w_lo, u + 1)
                for k in range(2):
                    kd = 2 * i + k
                    last = three(tile_bank(t), tokens(hTh, kd, c % NA, b, part), tokens(hTl, kd, c % NA, b, part),
                                 wview(u, False)[:, k, :], wview(u, True)[:, k, :], kd == 0, kd == KD - 1)
                if i == 3:
                    last.then_inc(proj_done, 1)
                elif b == TB - 1:
                    last.then_inc(w_used, 1)

            def first_gate(t, i):
                hf, u = t - NT, unit_of[("Y", 0)]
                if i == 0:
                    pe.wait_ge(w_lo, u + 1)
                    pe.wait_ge(qn_done, qk_number(*tile_at(bank_before(t))) + 1)
                wh, wl = wview(u, False), wview(u, True)
                for kd in (2 * i, 2 * i + 1):
                    last = three(bank(hf), wh[:, kd, :], wl[:, kd, :], tok(hTh)(kd, hf), tok(hTl)(kd, hf),
                                 kd == 0, kd == KD - 1)
                if (hf, i) == (1, 3):
                    last.then_inc(yg_done, 1)

            def transpose_qk(t):
                c, part, b = tile_at(t)
                n = qk_number(c, part, b)
                pe.wait_ge(rope_done, n + 1)
                if n:
                    pe.wait_ge(qkT_done, n)
                if part == K and b == 1 and c:
                    pe.wait_ge(st_evac, c)
                for h in range(HALF):
                    last = nc.tensor.transpose(bank(2)[:, P * h:P * h + P], qn[:, n % 2, P * h:P * h + P], ident[:, :])
                last.then_inc(qt_done, 1)

            def scores(n):
                c, h, b = block_at(n)
                pe.wait_ge(qkT_done, qk_number(c, Q, b) + 1)
                if n >= 2:
                    pe.wait_ge(masked, n - 1)
                k0, kn = key_cols(c % NA, b)
                nc.tensor.matmul(bank(5 + n % 2)[:, 0:kn], qT[:, b % 2, h, :], kT[:, h, k0:k0 + kn],
                                 start=True, stop=True).then_inc(s_done, 1)

            def transpose_p(n):
                c, h, b = block_at(n)
                pe.wait_ge(p_done, n + 1)
                if n >= 2:
                    pe.wait_ge(pt_ready, n - 1)
                for i in range(key_cols(c % NA, b)[1] // P):
                    last = nc.tensor.transpose(bank(3 + n % 2)[:, P * i:P * i + P], pp[:, n % 2, P * i:P * i + P],
                                               ident[:, :])
                last.then_inc(ptr_done, 1)

            def values(n):
                c, h, b = block_at(n)
                if b == 0 and h == 0:
                    pe.wait_ge(v_done, TB * (c + 1))
                pe.wait_ge(pt_ready, n + 1)
                if h == 0 and n:
                    pe.wait_ge(u_evac, n // HALF)
                vb = value_blocks(c % NA, b)
                for i, v in enumerate(vb):
                    last = nc.tensor.matmul(bank(7)[:, P * h:P * h + P], vv[:, v, HD * h:HD * h + HD],
                                            pt[:, n % 2, P * i:P * i + P], start=(i == 0), stop=(i == len(vb) - 1))
                last.then_inc(pv_done, 1)

            pe.wait_ge(o_added, 2 * TB * NG)
            for t in range(TB // 2):
                pe.wait_ge(hlo_done, TB + t + 1)
                for i in range(4):
                    project(t, i)
                transpose_x(1, TB // 2 + t)
            for t in range(TB // 2, NT + 3):
                for i, (s, tp, pv) in enumerate(slots(t)):
                    if t < NT:
                        if t <= TB // 2 + 1 and i == 0:
                            pe.wait_ge(hlo_done, TB + t + 1 if t == TB // 2 else 2 * TB)
                        project(t, i)
                    elif t < NT + 2:
                        first_gate(t, i)
                    if i == 1 and transposed_in(t) is not None:
                        transpose_qk(transposed_in(t))
                    if s is not None:
                        scores(s)
                    if tp is not None:
                        transpose_p(tp)
                    if pv is not None:
                        values(pv)
                if attended(t) is None and attended(t - 1) is not None:
                    pe.wait_ge(qkT_done, qk_number(*tile_at(min(t - 2, NT - 1))) + 1)
                    nc.tensor.transpose(bank(2)[0:2 * HALF * TB, 0:P],
                                        stat[:, :, :, :].rearrange("p s h b -> p (s h b)"),
                                        ident[:, :]).then_inc(stT_done, 1)
                if 1 <= t <= NT and tile_at(t - 1)[1] == Q:
                    transpose_qk(t - 1)

            for h in range(1, H):
                u = unit_of[("Y", h)]
                pe.wait_ge(w_lo, u + 1)
                if h == 1:
                    pe.wait_ge(st_evac, NCHUNK)
                elif h == 3:
                    pe.wait_ge(u_evac, NCHUNK * TB)
                elif h > 3:
                    pe.wait_ge(ysilu_done, h - 3)
                last = features_by_tokens(u, h % 4, KD, tok(hTh), tok(hTl))
                last.then_inc(yg_done, 1)
            def project_out(n, hh):
                hf, tb = n // TB, n % TB
                i, k = hh // 2, hh % 2
                u = unit_of[("Z", hf, i)]
                if tb == 0 and k == 0:
                    pe.wait_ge(w_lo, u + 1)
                last = three(bank(n % 4), yh[:, hh, P * tb:P * tb + P], yl[:, hh, P * tb:P * tb + P],
                             wview(u, False)[:, k, :], wview(u, True)[:, k, :], hh == 0, hh == H - 1)
                if hh == H - 1:
                    last.then_inc(z1_done, 1)
                elif tb == TB - 1 and k:
                    last.then_inc(w_used, 1)

            pe.wait_ge(ysilu_done, H - 2)
            for hh in range(H):
                pe.wait_ge(y_done, 2 * hh + 1)
                for n in range(4):
                    project_out(n, hh)
            pe.wait_ge(y_done, 2 * H)
            for n in range(4, 2 * TB):
                pe.wait_ge(out_ready, n - 3)
                for hh in range(H):
                    project_out(n, hh)

        @block.vector
        def _(dve):
            steps = [0]

            def link(ins):
                steps[0] += 1
                ins.then_inc(dve_step, 1)
                dve.wait_ge(dve_step, steps[0])

            def root_guess(v, y):
                link(nc.vector.tensor_scalar(y.bitcast(I32), v.bitcast(I32), -0.5, float(0x5F3759DF),
                                             ALU.mult, ALU.add))

            def newton(v, t, y, steps):
                for _ in range(steps):
                    link(nc.vector.scalar_tensor_tensor(out=t, in0=y, scalar=-0.5, in1=y, op0=ALU.mult, op1=ALU.mult))
                    link(nc.vector.tensor_tensor(t, t, v, ALU.mult))
                    link(nc.vector.scalar_tensor_tensor(out=y, in0=t, scalar=1.5, in1=y, op0=ALU.add, op1=ALU.mult))

            def add_out(g, po, tbs=range(TB)):
                for tb in tbs:
                    n = 2 * TB * g + TB * po + tb
                    dve.wait_ge(o_done, n + 1)
                    nc.vector.tensor_tensor(xs[:, tb, :], pair[pair_of[("O", g, po, tb)]][:, :], xs[:, tb, :],
                                            ALU.add).then_inc(o_added, 1)

            def norm_x(layer):
                def lows(tb):
                    n = layer * TB + tb
                    dve.wait_ge(hhi_done, n + 1)
                    nc.vector.tensor_tensor(hTl[:, :, P * tb:P * tb + P],
                                            pair[3][:, :].rearrange("p (k c) -> p k c", k=KD),
                                            hTh[:, :, P * tb:P * tb + P].bitcast(F32), ALU.subtract).then_inc(hlo_done, 1)

                def roots(first, end):
                    dve.wait_ge(sq_done, layer * TB + end)
                    c = slice(first, end)
                    link(nc.vector.tensor_scalar(var[:, c], ss[:, c], 1.0 / D, EPS, ALU.mult, ALU.add))
                    root_guess(var[:, c], rstd[:, c])
                    newton(var[:, c], tmp[:, c], rstd[:, c], 3)

                def scale(tb):
                    if tb >= 2:
                        dve.wait_ge(xt_done, layer * TB + tb - 1)
                    nc.vector.scalar_tensor_tensor(out=(bufU, bufS)[tb % 2][:, 0:D], in0=xs[:, tb, :],
                                                   scalar=rstd[:, tb:tb + 1], in1=bufG[:, :], op0=ALU.mult,
                                                   op1=ALU.mult).then_inc(xn_done, 1)

                def add(*tbs):
                    if layer:
                        add_out(NG - 1, 1, tbs)

                add(0)
                dve.wait_ge(nw_in, 16 * (layer + 1))
                roots(0, 1)
                scale(0)
                add(1)
                roots(1, 2)
                scale(1)
                lows(0)
                add(2, 3)
                roots(2, 4)
                scale(2)
                lows(1)
                scale(3)
                add(4, 5)
                roots(4, 6)
                lows(2)
                add(6, 7)
                scale(4)
                lows(3)
                scale(5)
                roots(6, 8)
                lows(4)
                scale(6)
                lows(5)
                scale(7)
                lows(6)
                lows(7)
                if layer == 1:
                    dve.wait_ge(hlo_done, TB + 1)
                    nc.vector.tensor_copy(hTl[:, :, T:TPAD], hTl[:, :, 0:SIDE].bitcast(F32)).then_inc(hpad_done, 1)

            norm_x(0)
            dve.wait_ge(const_in, 16 * 2)

            def pool_block(g, c):
                n = GB * g + c
                w = WINDOWS[g]
                dve.wait_ge(u_copied, n + 1)
                src, dst, k = bufU, bufS, 1
                while k < w:
                    ext = w // 2 - k
                    lo, num = PAD - ext, T + 2 * ext
                    s = max(k // 2, 1)
                    a, b = (-1, 0) if k == 1 else (-s, s)
                    link(nc.vector.tensor_tensor(dst[:, lo:lo + num], src[:, lo + a:lo + a + num],
                                                 src[:, lo + b:lo + b + num], ALU.add))
                    src, dst, k = dst, src, 2 * k
                ends = src[:, PAD:PAD + T].rearrange("p (a b) -> p a b", b=8)[:, 0:TB * 16:TB * 16 - 1, :]
                link(nc.vector.tensor_tensor(ends, ends, edge[:, g, :, :], ALU.mult))
                mid = src[:, PAD:PAD + T]
                nc.vector.scalar_tensor_tensor(out=mid, in0=mid, scalar=1.0 / w, in1=pair[pair_of[("U", g, c)]][:, :],
                                               op0=ALU.mult, op1=ALU.subtract).then_inc(d_ready, 1)
                dve.wait_ge(dhi_done, n + 1)
                nc.vector.tensor_tensor(diffl[:, c, :], mid, diffh[:, c, :].bitcast(F32),
                                        ALU.subtract).then_inc(diff_done, 1)
                if w >= 8:
                    link(nc.vector.memset(bufU[:, 0:PAD], 0.0))
                    link(nc.vector.memset(bufU[:, PAD + T:], 0.0))

            def z_block(g, c):
                n = GB * g + c
                dve.wait_ge(silu_done, n + 1)
                dve.wait_ge(m_done, n + 1)
                nc.vector.scalar_tensor_tensor(out=bufG[:, :], in0=pair[pair_of[("M", g, c)]][:, :],
                                               scalar=pscale[:, n:n + 1], in1=bufG[:, :], op0=ALU.mult,
                                               op1=ALU.mult).then_inc(z_ready, 1)
                dve.wait_ge(zhi_done, n + 1)
                nc.vector.tensor_tensor(zl[:, c % 2, :], bufG[:, :], zh[:, c % 2, :].bitcast(F32),
                                        ALU.subtract).then_inc(z_done, 1)

            dve.wait_ge(xt_done, TB)
            link(nc.vector.memset(bufU[:, 0:PAD], 0.0))
            link(nc.vector.memset(bufU[:, PAD + T:], 0.0))
            for g in range(NG):
                pool_block(g, 0)
                if g:
                    add_out(g - 1, 1)
                for c in range(1, GB):
                    pool_block(g, c)
                z_block(g, 0)
                z_block(g, 1)
                add_out(g, 0)
                z_block(g, 2)
                z_block(g, 3)
            norm_x(1)
            dve.wait_ge(x1_out, 16 * TB)
            dve.wait_ge(acon_in, 16 * 9)
            dve.wait_ge(xn_done, 2 * TB)
            nc.vector.memset(kT[:, :, 0:SIDE], 0.0).then_inc(kpad_set, 1)
            nc.vector.memset(kT[:, :, SIDE + T:], 0.0).then_inc(kpad_set, 1)
            nc.vector.memset(wcol[0:ROPE, :], 1.0).then_inc(wcol_set, 1)

            def fold(g, part):
                i = NA * (part == K) + g
                hr = ROPE // 2
                w = wrow[:, i, :].unsqueeze(1)
                nc.vector.tensor_tensor(cosw[:, :, :], cosb[:, g, :, :], w.to_broadcast([P, TB, ROPE]), ALU.mult)
                nc.vector.tensor_tensor(sinw[:, :, 0:hr], sinb[:, g, :, 0:hr],
                                        w[:, :, hr:].to_broadcast([P, TB, hr]), ALU.mult)
                link(nc.vector.tensor_tensor(sinw[:, :, hr:], sinb[:, g, :, hr:],
                                             w[:, :, 0:hr].to_broadcast([P, TB, hr]), ALU.mult))

            def mean_square(t):
                n = qk_number(*tile_at(t))
                x4 = qn[:, n % 2, :].rearrange("p (h e) -> p h e", h=HALF)
                dve.wait_ge(qsq_done, n + 1)
                link(nc.vector.tensor_reduce(qss[:, :], x4, AX_X, ALU.add))
                link(nc.vector.tensor_scalar(qvar[:, :], qss[:, :], 1.0 / HD, EPS, ALU.mult, ALU.add))
                root_guess(qvar[:, :], qrstd[:, :])
                newton(qvar[:, :], qtmp[:, :], qrstd[:, :], 1)

            def inverse_root(t):
                newton(qvar[:, :], qtmp[:, :], qrstd[:, :], 2)

            def norm_and_rotate(t):
                n = qk_number(*tile_at(t))
                x4 = qn[:, n % 2, :].rearrange("p (h e) -> p h e", h=HALF)
                nc.vector.tensor_tensor(x4, tile_bank(t).rearrange("p (h e) -> p h e", h=HALF),
                                        qrstd[:, :].unsqueeze(2).to_broadcast([P, HALF, HD]),
                                        ALU.mult).then_inc(qn_done, 1)
                dve.wait_ge(qn_done, n + 1)
                b = t % TB
                hr = ROPE // 2
                cw, sw = cosw[:, b, :].unsqueeze(1), sinw[:, b, :].unsqueeze(1)
                nc.vector.tensor_tensor(ropeA[:, :, :], x4[:, :, 0:ROPE], cw.to_broadcast([P, HALF, ROPE]), ALU.mult)
                nc.vector.tensor_tensor(ropeB[:, :, 0:hr], x4[:, :, hr:ROPE],
                                        sw[:, :, 0:hr].to_broadcast([P, HALF, hr]), ALU.mult)
                link(nc.vector.tensor_tensor(ropeB[:, :, hr:], x4[:, :, 0:hr],
                                             sw[:, :, hr:].to_broadcast([P, HALF, hr]), ALU.mult))
                nc.vector.tensor_tensor(x4[:, :, 0:ROPE], ropeA[:, :, :], ropeB[:, :, :], ALU.add).then_inc(rope_done, 1)

            def row_max(n):
                c, h, b = block_at(n)
                kn = key_cols(c % NA, b)[1]
                dve.wait_ge(s_done, n + 1)
                if n >= 2:
                    dve.wait_ge(ptr_done, n - 1)
                if b == 0 and h == 0 and c:
                    dve.wait_ge(stT_done, c)
                nc.vector.tensor_tensor_reduce(pp[:, n % 2, 0:kn], bank(5 + n % 2)[:, 0:kn], mask_of(c % NA, b), -SCALE,
                                               3e38, ALU.add, ALU.min, stat[:, 0, h, b:b + 1]).then_inc(masked, 1)

            def take_pt(n):
                c, h, b = block_at(n)
                kn = key_cols(c % NA, b)[1]
                dve.wait_ge(ptr_done, n + 1)
                if n >= 2:
                    dve.wait_ge(pv_done, n - 1)
                nc.vector.tensor_copy(pt[:, n % 2, 0:kn], bank(3 + n % 2)[:, 0:kn]).then_inc(pt_ready, 1)

            def grouped(t, g):
                if g == 0:
                    return t[:, g, :]
                return t[:, g, :].rearrange("p (r j) -> p j r", r=STRIDE[g])

            def natural(t2, g):
                return t2 if g == 0 else t2.rearrange("p (j r) -> p j r", r=STRIDE[g])

            def factors(half):
                dve.wait_ge(f_in, 16 * 2 * (1 + (NA - 1) * HALF) * (half + 1))
                link(nc.vector.tensor_copy(ftot, fm[:, 0, :]))
                for g in (1, 2):
                    link(nc.vector.tensor_tensor(natural(ftot, g), natural(ftot, g), grouped(fm, g), ALU.min))
                for g in range(NA):
                    link(nc.vector.tensor_tensor(grouped(fm, g), natural(ftot, g), grouped(fm, g), ALU.subtract))
                nc.vector.memset(ftot, 0.0).then_inc(f_sub, 1)
                dve.wait_ge(f_exp, half + 1)
                dve.wait_ge(f_sub, half + 1)
                for g in range(NA):
                    link(nc.vector.tensor_tensor(fden[:, g, :], fden[:, g, :], fm[:, g, :], ALU.mult))
                    link(nc.vector.tensor_tensor(natural(ftot, g), natural(ftot, g), grouped(fden, g), ALU.add))
                link(nc.vector.reciprocal(ftot, ftot))
                for g in range(NA):
                    last = nc.vector.tensor_tensor(natural(fden[:, g, :], g), grouped(fm, g), natural(ftot, g),
                                                   ALU.mult)
                last.then_inc(f_ready, 1)

            def merge(m):
                buf, arrived, n = merge_buffer(m)
                dve.wait_ge(arrived, n)
                for g in range(NA):
                    if g == 0:
                        a, f = buf[:, 0, :], buf[:, NA, :]
                    else:
                        a = buf[:, g, :].rearrange("p (r j) -> p j r", r=STRIDE[g])
                        f = buf[:, NA + g, :].rearrange("p (j r) -> p j r", r=STRIDE[g])
                    op = nc.vector.tensor_tensor(f, a, f, ALU.mult)
                link(op)
                h, hf = m // 2, m % 2
                out = uf[:, 0, :] if m < H else mixed[:, h, 512 * hf:512 * hf + 512]
                link(nc.vector.tensor_tensor(buf[:, NA, :], buf[:, NA, :], buf[:, NA + 1, :], ALU.add))
                nc.vector.tensor_tensor(out, buf[:, NA, :], buf[:, NA + 2, :], ALU.add).then_inc(merged, 1)

            for t in range(NT + 3):
                c, part, b = tile_at(t - 1) if 1 <= t <= NT else (0, V, 1)
                stages = []
                if part != V:
                    if b == 0:
                        fold(c % NA, part)
                    stages = [mean_square, inverse_root, norm_and_rotate]
                for i, (s, tp, pv) in enumerate(slots(t)):
                    if s is not None:
                        row_max(s)
                    if tp is not None:
                        take_pt(tp)
                    if i < len(stages):
                        stages[i](t - 1)
                if t == factor_step:
                    factors(0)
                if t in merge_at:
                    merge(merge_at[t])

            factors(1)
            dve.wait_ge(pv_done, NCHUNK * TB * HALF)
            dve.wait_ge(st_out, 16 * 2 * NCHUNK)
            for i in range(2):
                dve.wait_ge(u_out[i], 16 * NCHUNK * TB // 2)
            for h in range(H):
                if h < HALF:
                    merge(H + 2 * h)
                    merge(H + 2 * h + 1)
                    dve.wait_ge(o_in[h], 16)
                else:
                    dve.wait_ge(merged, 2 * h + 2)
                dve.wait_ge(ysilu_done, h + 1)
                if h:
                    dve.wait_ge(y_done, 2 * h)
                for hf in range(2):
                    tok_half = slice(512 * hf, 512 * hf + 512)
                    nc.vector.tensor_tensor(yo[:, hf, :], mixed[:, h, tok_half], gate[:, h, tok_half],
                                            ALU.mult).then_inc(y_ready, 1)
                for hf in range(2):
                    tok_half = slice(512 * hf, 512 * hf + 512)
                    dve.wait_ge(yhi_done, 2 * h + hf + 1)
                    nc.vector.tensor_tensor(yl[:, h, tok_half], yo[:, hf, :], yh[:, h, tok_half].bitcast(F32),
                                            ALU.subtract).then_inc(y_done, 1)

            for n in range(2 * TB):
                dve.wait_ge(x1_in[n % 3], 16 * (n // 3 + 1))
                dve.wait_ge(z1_done, n + 1)
                s = n % 3
                nc.vector.tensor_tensor(uf[:, s, :], bank(n % 4), uf[:, s, :], ALU.add).then_inc(out_ready, 1)

        @block.scalar
        def _(act):
            act.dma_start(xs[:, 0, :], x2[0:P, :]).then_inc(xin[0], 16)
            act.dma_start(bufG[:, :], pool_norm[0:1, :].to_broadcast([P, D])).then_inc(nw_in, 16)
            act.dma_start(ident[:, :], ident_d).then_inc(ident_in, 16)
            for tb in range(1, 3):
                act.dma_start(xs[:, tb, :], x2[P * tb:P * tb + P, :]).then_inc(xin[tb], 16)
            act.dma_start(pscale[:, :], pool_scale[0].rearrange("(c p) -> p c", p=P),
                          allow_slow_non_contiguous=True).then_inc(const_in, 16)
            act.dma_start(edge[:, :, :, :].rearrange("p g a b -> p (g a b)"),
                          edge_d.to_broadcast([P, NG * 16])).then_inc(const_in, 16)

            def load_tables():
                act.dma_start(cosb[:, :, :, :], cos_d.rearrange("g (b p) e -> p g b e", p=P)).then_inc(acon_in, 16)
                act.dma_start(sinb[:, :, :, :], sin_d.rearrange("g (b p) e -> p g b e", p=P)).then_inc(acon_in, 16)
                wr = wrow[:, :, :].rearrange("p (k g) e -> p k g e", k=2)
                wc = wcol[ROPE:P, :].rearrange("p (k g) -> p k g", k=2)
                for k, w in enumerate((att_q_norm, att_k_norm)):
                    act.dma_start(wr[:, k], w[0:1, :, 0:ROPE].to_broadcast([P, NA, ROPE])).then_inc(acon_in, 16)
                    act.dma_start(wc[:, k], w[0, :, ROPE:HD].rearrange("g e -> e g"),
                                  allow_slow_non_contiguous=True).then_inc(acon_in, 16)
                act.dma_start(mask0[:, :, :], mask0_d.rearrange("m p c -> p m c")).then_inc(acon_in, 16)
                act.dma_start(mask1[:, :, :], mask1_d.rearrange("m p c -> p m c")).then_inc(acon_in, 16)
                act.dma_start(mask2[:, :], mask2_d).then_inc(acon_in, 16)

            def norm_x(layer):
                def highs(tb):
                    n = layer * TB + tb
                    act.wait_ge(xt_done, n + 1)
                    nc.scalar.activation(hTh[:, :, P * tb:P * tb + P],
                                         pair[3][:, :].rearrange("p (k c) -> p k c", k=KD),
                                         ACT.Copy).then_inc(hhi_done, 1)

                def square(tb):
                    n = layer * TB + tb
                    if layer == 0:
                        act.wait_ge(xin[tb], 16)
                        if tb + 3 < TB:
                            act.dma_start(xs[:, tb + 3, :], x2[P * (tb + 3):P * (tb + 4), :]).then_inc(xin[tb + 3], 16)
                    else:
                        act.wait_ge(o_added, 2 * TB * NG - TB + tb + 1)
                        act.dma_start(x1_d[P * tb:P * tb + P, :], xs[:, tb, :]).then_inc(x1_out, 16)
                        if tb == 6:
                            act.wait_ge(o_added, 2 * TB * NG)
                            load_tables()
                    if n:
                        act.wait_ge(sq_done, n)
                    nc.scalar.activation(squares[:, :], xs[:, tb, :], ACT.Square,
                                         accum_out=ss[:, tb:tb + 1]).then_inc(sq_done, 1)

                square(0)
                square(1)
                highs(0)
                square(2)
                square(3)
                highs(1)
                square(4)
                square(5)
                highs(2)
                highs(3)
                square(6)
                square(7)
                for tb in range(4, TB):
                    highs(tb)
                if layer == 1:
                    act.wait_ge(hhi_done, TB + 1)
                    nc.scalar.activation(hTh[:, :, T:TPAD], hTh[:, :, 0:SIDE].bitcast(F32),
                                         ACT.Copy).then_inc(hpad_done, 1)

            act.wait_ge(zero_set, 1)
            nc.scalar.activation(squares[:, 0:1], zero[:, :], ACT.Square).then_inc(table_loaded, 1)
            act.wait_ge(table_loaded, 1)
            norm_x(0)
            for g in range(NG):
                for c in range(GB):
                    n = GB * g + c
                    act.wait_ge(u_done, n + 1)
                    if n == 0:
                        act.wait_ge(xt_done, TB)
                    else:
                        act.wait_ge(diff_done, n)
                    nc.scalar.activation(bufU[:, PAD:PAD + T], pair[pair_of[("U", g, c)]][:, :],
                                         ACT.Copy).then_inc(u_copied, 1)
                    act.wait_ge(d_ready, n + 1)
                    if g:
                        act.wait_ge(m_done, GB * g)
                    fin = bufU if g % 2 else bufS
                    nc.scalar.activation(diffh[:, c, :], fin[:, PAD:PAD + T], ACT.Copy).then_inc(dhi_done, 1)
                for c in range(GB):
                    n = GB * g + c
                    act.wait_ge(g_done, n + 1)
                    if n == 0:
                        act.wait_ge(xn_done, TB)
                    else:
                        act.wait_ge(z_done, n)
                    nc.scalar.activation(bufG[:, :], pair[pair_of[("G", g, c)]][:, :], ACT.Silu).then_inc(silu_done, 1)
                    act.wait_ge(z_ready, n + 1)
                    if n >= 2:
                        act.wait_ge(o_done, 2 * TB * ((n - 2) // GB) + TB * ((n - 2) % GB // 2) + TB)
                    nc.scalar.activation(zh[:, c % 2, :], bufG[:, :], ACT.Copy).then_inc(zhi_done, 1)

            act.wait_ge(z_done, GB * NG)
            act.dma_start(bufG[:, :], att_norm[0:1, :].to_broadcast([P, D])).then_inc(nw_in, 16)
            norm_x(1)
            act.wait_ge(x1_out, 16 * TB)
            act.wait_ge(acon_in, 16 * 9)
            act.wait_ge(wcol_set, 1)
            act.wait_ge(kpad_set, 2)

            def square(t):
                n = qk_number(*tile_at(t))
                act.wait_ge(proj_done, t + 1)
                if n >= 2:
                    act.wait_ge(qt_done, n - 1)
                nc.scalar.activation(qn[:, n % 2, :], tile_bank(t), ACT.Square).then_inc(qsq_done, 1)

            def take_qk(t):
                c, part, b = tile_at(t)
                n = qk_number(c, part, b)
                act.wait_ge(qt_done, n + 1)
                if part == Q:
                    if n >= 2 and TB * c + b >= 2:
                        act.wait_ge(s_done, HALF * (TB * c + b - 1))
                    dst = qT[:, b % 2, :, :]
                else:
                    if b == 0 and c:
                        act.wait_ge(s_done, HALF * TB * c)
                    dst = kT[:, :, SIDE + P * b:SIDE + P * b + P]
                i = NA * (part == K) + c % NA
                nc.scalar.activation(dst, bank(2).rearrange("p (h t) -> p h t", h=HALF), ACT.Copy,
                                     scale=wcol[:, i:i + 1]).then_inc(qkT_done, 1)

            def take_v(t):
                c, part, b = tile_at(t)
                act.wait_ge(proj_done, t + 1)
                if b == 0 and c:
                    act.wait_ge(pv_done, HALF * TB * c)
                nc.scalar.activation(vv[:, b, :], tile_bank(t), ACT.Copy).then_inc(v_done, 1)

            def exps(n):
                c, h, b = block_at(n)
                kn = key_cols(c % NA, b)[1]
                act.wait_ge(masked, n + 1)
                nc.scalar.activation(pp[:, n % 2, 0:kn], pp[:, n % 2, 0:kn], ACT.Exp, bias=stat[:, 0, h, b:b + 1],
                                     scale=-1.0, accum_out=stat[:, 1, h, b:b + 1]).then_inc(p_done, 1)

            def take_u(a):
                c, b = a // TB, a % TB
                act.wait_ge(pv_done, HALF * (a + 1))
                if a >= 2:
                    act.wait_ge(u_out[a % 2], 16 * (a // 2))
                nc.scalar.activation(uo[:, a % 2, :, :], bank(7).rearrange("p (h t) -> p h t", h=HALF),
                                     ACT.Copy).then_inc(u_evac, 1)
                act.wait_ge(u_evac, a + 1)
                h0 = HALF * (c // NA)
                act.dma_start(u_d[c % NA, h0:h0 + HALF, :, P * b:P * b + P].rearrange("h e t -> e h t"),
                              uo[:, a % 2, :, :]).then_inc(u_out[a % 2], 16)

            def take_stat(c):
                act.wait_ge(stT_done, c + 1)
                if c:
                    act.wait_ge(st_out, 16 * 2 * c)
                nc.scalar.activation(statT[:, :], bank(2)[0:2 * HALF * TB, 0:P], ACT.Copy).then_inc(st_evac, 1)
                act.wait_ge(st_evac, c + 1)
                half, g = c // NA, c % NA
                for s in range(2):
                    act.dma_start(st_d[g, s, HALF * half:HALF * half + HALF].rearrange("h (b q) -> (h b) q", q=P),
                                  statT[s * HALF * TB:(s + 1) * HALF * TB, :]).then_inc(st_out, 16)

            def exp_factors(half):
                act.wait_ge(f_sub, half + 1)
                nc.scalar.activation(fm, fm, ACT.Exp).then_inc(f_exp, 1)

            for t in range(NT + 3):
                if 2 <= t <= NT + 1 and tile_at(t - 2)[1] == Q:
                    take_qk(t - 2)
                part = tile_at(t - 1)[1] if 1 <= t <= NT else None
                if part == V:
                    take_v(t - 1)
                elif part is not None:
                    square(t - 1)
                if 2 <= t <= NT + 1 and tile_at(t - 2)[1] == K:
                    take_qk(t - 2)
                z = attended(t - 1)
                for i, (s, tp, pv) in enumerate(slots(t)):
                    if i == 2 and z is not None:
                        take_u(z)
                    if s is not None:
                        exps(s)
                if attended(t) is None and z is not None:
                    take_stat(z // TB)
                if t == factor_step:
                    exp_factors(0)
                if t + 1 < NT and (t + 1) % TB == 0:
                    c, part, _ = tile_at(t + 1)
                    u = unit_of[("A", c, part, 3)]
                    if u in act_units:
                        act.wait_ge(raw_in[u % RAW], 16 * (u // RAW + 1))
                        act.wait_ge(*unit_released(u - R1))
                        nc.scalar.activation(w1[:, slot(u), 0, :], raw[:, u % RAW, :], ACT.Copy).then_inc(w_hi_act, 1)

            exp_factors(1)
            act.wait_ge(u_out[0], 16 * NCHUNK * TB // 2)
            act.wait_ge(u_out[1], 16 * NCHUNK * TB // 2)
            act.wait_ge(st_out, 16 * 2 * NCHUNK)
            act.wait_ge(o_out, 16 * H)
            for h in range(HALF):
                act.dma_start(mixed[:, h, :], o_d[h]).then_inc(o_in[h], 16)

            def load_x1(n):
                if n >= 3:
                    act.wait_ge(out_sent[n % 3], 16 * (n // 3))
                act.dma_start(uf[:, n % 3, :], tile(x1_d, n)).then_inc(x1_in[n % 3], 16)

            def tile(t, n):
                hf, tb = n // TB, n % TB
                return t[P * tb:P * tb + P, 512 * hf:512 * hf + 512]

            for h in range(H):
                act.wait_ge(yg_done, h + 1)
                if h == H - 3:
                    act.wait_ge(merged, 2 * H)
                    for n in range(2):
                        load_x1(n)
                nc.scalar.activation(gate[:, h, :], pair[h % 4][:, :], ACT.Silu).then_inc(ysilu_done, 1)
                for hf in range(2):
                    act.wait_ge(y_ready, 2 * h + hf + 1)
                    nc.scalar.activation(yh[:, h, 512 * hf:512 * hf + 512], yo[:, hf, :], ACT.Copy).then_inc(yhi_done, 1)

            for n in range(2 * TB + 1):
                if 2 <= n < 2 * TB:
                    load_x1(n)
                if n >= 1:
                    act.wait_ge(out_ready, n)
                    act.dma_start(tile(out2, n - 1), uf[:, (n - 1) % 3, :]).then_inc(out_sent[(n - 1) % 3], 16)
            for i in range(3):
                act.wait_ge(out_sent[i], 16 * len(range(i, 2 * TB, 3)))


_INS = ["x", "pool_norm", "pool_w_in", "pool_w_group", "pool_scale", "pool_w_out", "att_norm", "att_w_in",
        "att_q_norm", "att_k_norm", "att_w_out"]


def shape_constants(T):
    import numpy as np
    neg = np.float32(-1e30)
    ident = np.eye(P, dtype=np.float32)
    q, c = np.arange(P)[:, None], np.arange(256)[None, :]
    band = (c - q >= 0) & (c - q <= 2 * SIDE)
    ok0 = np.stack([band & (c >= SIDE), band, band & (c < 256 - SIDE)])
    ok1 = np.stack([np.abs(c - (P * b + q)) <= SIDE for b in range(2)])
    ok2 = (q % 2) == (c[:, :P] % 2)
    masks = [np.where(m, np.float32(0), neg).astype(np.float32) for m in (ok0, ok1, ok2)]
    half = ROPE // 2
    f32 = np.float32
    inv = (f32(1.0) / (f32(500000.0) ** (np.arange(half, dtype=f32) * f32(2.0) / f32(ROPE)))).astype(f32)
    ang = np.arange(T, dtype=f32)[:, None] * inv[None, :]
    cos, sin = np.cos(ang).astype(f32), np.sin(ang).astype(f32)
    edge = np.ones((len(WINDOWS), 2, 8), f32)
    for g, w in enumerate(WINDOWS):
        for i, t in enumerate(list(range(8)) + list(range(T - 8, T))):
            n = min(t - w // 2 + w, T) - max(t - w // 2, 0)
            edge[g, i // 8, i % 8] = f32(w / n)
    order = [np.arange(T).reshape(T // r, r).T.ravel() for r in STRIDE]
    cos, sin = (np.stack([a[o] for o in order]) for a in (cos, sin))
    return {"ident": ident, "mask0": masks[0], "mask1": masks[1], "mask2": masks[2],
            "cos": np.concatenate([cos, cos], 2), "sin": np.concatenate([-sin, sin], 2),
            "edge": edge.reshape(1, -1)}


def kernel(**inputs):
    import numpy as np
    import concourse.bacc as bacc
    from concourse.bass_utils import run_bass_kernel_spmd as run

    nc = bacc.Bacc("TRN2", target_bir_lowering=False, num_devices=1)
    arrays, args = {}, []
    given = {n: np.ascontiguousarray(inputs[n]) for n in _INS}
    given.update(shape_constants(inputs["x"].shape[1]))
    for name, a in given.items():
        arrays[f"in_{name}_dram"] = a
        args.append(nc.dram_tensor(f"in_{name}_dram", a.shape, mybir.dt.from_np(a.dtype), kind="ExternalInput").ap())
    shape = inputs["x"].shape
    args.append(nc.dram_tensor("out_dram", shape, F32, kind="ExternalOutput").ap())
    encoder_program(nc, *args)
    r = run(nc, [arrays], core_ids=[0])
    return r.results[0]["out_dram"]
```
